# Optimizing a Trainium2 kernel written in Bass

```python
import jax
import jax.numpy as jnp
from jax import lax
import numpy as np

D_MODEL = 1024
BATCH = 1
SEQ = 256
DEPTH = 2

N_META = 16
LEAD = 128
PAD = LEAD - N_META
Q_BLOCK = 128
CHUNK = 64
EPS = 1e-6
NEG_INF = -1e30

MLA_HEADS = 8
MLA_Q_LORA = 256
MLA_KV_LORA = 128
MLA_NOPE = 64
MLA_ROPE = 32
MLA_V = 64
MLA_QK = MLA_NOPE + MLA_ROPE
MLA_VW = MLA_HEADS * MLA_V
ROPE_THETA = 10000.0

GLA_HEADS = 4
GLA_DK = 64
GLA_DV = 128
GLA_KW = GLA_HEADS * GLA_DK
GLA_VW = GLA_HEADS * GLA_DV
GLA_GATE_RANK = 16
GLA_GATE_NORM = 16.0

HGRN_HEADS = 4
HGRN_DK = 128
HGRN_DV = 128
HGRN_KW = HGRN_HEADS * HGRN_DK
HGRN_VW = HGRN_HEADS * HGRN_DV

N_BRANCH = 3
IN_SPLITS = (MLA_Q_LORA, MLA_KV_LORA, MLA_ROPE, GLA_KW, GLA_KW, GLA_VW, GLA_GATE_RANK, GLA_VW, HGRN_KW, HGRN_KW, HGRN_VW, HGRN_VW, N_BRANCH * D_MODEL)
IN_COLS = sum(IN_SPLITS)

D_FF = 2816
N_EXPERTS = 8
TOP_K = 2
D_EXPERT = 3584
MOE_BLOCK = 128
N_DENSE = (DEPTH + 1) // 2
N_MOE = DEPTH // 2

kernel_name = 'hybrid_mla_gla_hgrn2_moe_block'

def rmsnorm(x, g):
    xf = x.astype(jnp.float32)
    y = xf * lax.rsqrt(jnp.mean(xf * xf, axis=-1, keepdims=True) + EPS)
    return (y * g.astype(jnp.float32)).astype(x.dtype)

def rope(x, pos):
    half = x.shape[-1] // 2
    inv = ROPE_THETA ** (-jnp.arange(half, dtype=jnp.float32) / half)
    ang = pos.astype(jnp.float32)[:, None] * inv[None, :]
    cos = jnp.cos(ang)[None, :, None, :]
    sin = jnp.sin(ang)[None, :, None, :]
    xf = x.astype(jnp.float32)
    x1, x2 = xf[..., :half], xf[..., half:]
    return jnp.concatenate([x1 * cos - x2 * sin, x1 * sin + x2 * cos], axis=-1).astype(x.dtype)

def causal_block_attention(q, k, v):
    B, L, H, dq = q.shape
    padw = ((0, 0), (PAD, 0), (0, 0), (0, 0))
    qp, kp, vp = (jnp.pad(t, padw) for t in (q, k, v))
    Lp = L + PAD
    nb = Lp // Q_BLOCK
    key_pos = jnp.arange(Lp)
    key_ok = key_pos >= PAD
    q_blocks = qp.reshape(B, nb, Q_BLOCK, H, dq).transpose(1, 0, 2, 3, 4)
    scale = dq ** -0.5

    def attend(args):
        qb, i = args
        s = jnp.einsum('bqhd,bkhd->bhqk', qb, kp).astype(jnp.float32) * scale
        q_pos = i * Q_BLOCK + jnp.arange(Q_BLOCK)
        mask = (key_pos[None, :] <= q_pos[:, None]) & key_ok[None, :]
        p = jax.nn.softmax(jnp.where(mask, s, NEG_INF), axis=-1).astype(vp.dtype)
        return jnp.einsum('bhqk,bkhd->bqhd', p, vp)

    o = lax.map(attend, (q_blocks, jnp.arange(nb)))
    o = o.transpose(1, 0, 2, 3, 4).reshape(B, Lp, H, v.shape[-1])
    return o[:, PAD:]

def chunk_gated_linear_attention(q, k, v, log_g):
    dtype = v.dtype
    B, L, H, dk = q.shape
    dv = v.shape[-1]
    Lp = L + PAD
    N = Lp // CHUNK
    padw = ((0, 0), (PAD, 0), (0, 0), (0, 0))

    def to_chunks(t):
        return jnp.pad(t.astype(jnp.float32), padw).reshape(B, N, CHUNK, H, t.shape[-1])

    q, k, v, log_g = (to_chunks(t) for t in (q, k, v, log_g))
    b = jnp.cumsum(log_g, axis=2)
    b_ref = b[:, :, CHUNK // 2 - 1:CHUNK // 2]
    b_last = b[:, :, CHUNK - 1:CHUNK]
    causal = jnp.tril(jnp.ones((CHUNK, CHUNK), dtype=bool))
    a = jnp.einsum('bnihd,bnjhd->bnhij', q * jnp.exp(b - b_ref), k * jnp.exp(b_ref - b))
    a = jnp.where(causal, a, 0.0)
    o_intra = jnp.einsum('bnhij,bnjhv->bnihv', a, v)
    d_state = jnp.einsum('bnjhd,bnjhv->bnhdv', k * jnp.exp(b_last - b), v)
    decay = jnp.exp(b_last[:, :, 0])

    def step(S, inp):
        ds_n, dec_n = inp
        return dec_n[..., None] * S + ds_n, S

    _, s_prev = lax.scan(step, jnp.zeros((B, H, dk, dv), jnp.float32),
                         (jnp.moveaxis(d_state, 1, 0), jnp.moveaxis(decay, 1, 0)))
    s_prev = jnp.moveaxis(s_prev, 0, 1)
    o_inter = jnp.einsum('bnihd,bnhdv->bnihv', q * jnp.exp(b), s_prev)
    o = (o_intra + o_inter).reshape(B, Lp, H, dv)[:, PAD:]
    return o.astype(dtype)

def mla_branch(x_dq, x_dkv, x_kr, cq_norm, w_uq, ckv_norm, w_ukv, q_norm, k_norm):
    B, L, _ = x_dq.shape
    pos = jnp.arange(L, dtype=jnp.int32)
    q = (rmsnorm(x_dq, cq_norm) @ w_uq).reshape(B, L, MLA_HEADS, MLA_QK)
    kv = (rmsnorm(x_dkv, ckv_norm) @ w_ukv).reshape(B, L, MLA_HEADS, MLA_NOPE + MLA_V)
    k_rope = jnp.broadcast_to(x_kr[:, :, None, :], (B, L, MLA_HEADS, MLA_ROPE))
    k = jnp.concatenate([kv[..., :MLA_NOPE], k_rope], axis=-1)
    v = kv[..., MLA_NOPE:]
    q = rmsnorm(q, q_norm)
    k = rmsnorm(k, k_norm)
    q = jnp.concatenate([q[..., :MLA_NOPE], rope(q[..., MLA_NOPE:], pos)], axis=-1)
    k = jnp.concatenate([k[..., :MLA_NOPE], rope(k[..., MLA_NOPE:], pos)], axis=-1)
    return causal_block_attention(q, k, v).reshape(B, L, MLA_VW)

def gla_branch(x_q, x_k, x_v, x_gd, x_r, w_g2, b_g, o_norm):
    B, L, _ = x_q.shape
    log_g = jax.nn.log_sigmoid((x_gd @ w_g2 + b_g).astype(jnp.float32)) / GLA_GATE_NORM
    q = x_q.reshape(B, L, GLA_HEADS, GLA_DK) * (GLA_DK ** -0.5)
    k = x_k.reshape(B, L, GLA_HEADS, GLA_DK)
    v = x_v.reshape(B, L, GLA_HEADS, GLA_DV)
    o = chunk_gated_linear_attention(q, k, v, log_g.reshape(B, L, GLA_HEADS, GLA_DK))
    return rmsnorm(o, o_norm).reshape(B, L, GLA_VW) * jax.nn.silu(x_r)

def hgrn2_branch(x_q, x_f, x_i, x_g, lower_bound, o_norm):
    B, L, _ = x_q.shape
    f = lower_bound + (1.0 - lower_bound) * jax.nn.sigmoid(x_f.astype(jnp.float32))
    log_f = jnp.log(f)
    k = 1.0 - f
    q = jax.nn.silu(x_q)
    o = chunk_gated_linear_attention(q.reshape(B, L, HGRN_HEADS, HGRN_DK), k.reshape(B, L, HGRN_HEADS, HGRN_DK),
                                     x_i.reshape(B, L, HGRN_HEADS, HGRN_DV), log_f.reshape(B, L, HGRN_HEADS, HGRN_DK))
    return rmsnorm(o, o_norm).reshape(B, L, HGRN_VW) * jax.nn.silu(x_g)

def swiglu(u, w_gate, w_up, w_down):
    return (jax.nn.silu(u @ w_gate) * (u @ w_up)) @ w_down

def moe_swiglu(u, w_router, b_router, w_gate, w_up, w_down):
    B, L, D = u.shape
    T = B * L
    A = T * TOP_K
    xt = u.reshape(T, D)
    logits = (xt @ w_router + b_router).astype(jnp.float32)
    top_val, top_idx = lax.top_k(logits, TOP_K)
    gate = jax.nn.softmax(top_val, axis=-1)
    e_flat = top_idx.reshape(A)
    tok_flat = jnp.repeat(jnp.arange(T, dtype=jnp.int32), TOP_K)
    order = jnp.argsort(e_flat)
    e_sorted = e_flat[order]
    counts = jnp.bincount(e_flat, length=N_EXPERTS)
    start = jnp.cumsum(counts) - counts
    padded = (counts + MOE_BLOCK - 1) // MOE_BLOCK * MOE_BLOCK
    pend = jnp.cumsum(padded)
    pstart = pend - padded
    dest = pstart[e_sorted] + jnp.arange(A) - start[e_sorted]
    n_blocks = -(-A // MOE_BLOCK) + N_EXPERTS
    P = n_blocks * MOE_BLOCK
    slot_tok = jnp.zeros((P,), jnp.int32).at[dest].set(tok_flat[order])
    slot_w = jnp.zeros((P,), jnp.float32).at[dest].set(gate.reshape(A)[order])
    block_expert = jnp.minimum(jnp.searchsorted(pend, jnp.arange(n_blocks) * MOE_BLOCK, side='right'), N_EXPERTS - 1)

    def expert_block(args):
        tok, e = args
        xb = xt[tok]
        hb = jax.nn.silu(xb @ w_gate[e]) * (xb @ w_up[e])
        return hb @ w_down[e]

    y_slots = lax.map(expert_block, (slot_tok.reshape(n_blocks, MOE_BLOCK), block_expert))
    y_slots = y_slots.reshape(P, D) * slot_w[:, None].astype(u.dtype)
    return jnp.zeros((T, D), u.dtype).at[slot_tok].add(y_slots).reshape(B, L, D)

def setup_inputs(seed: int = 0) -> dict:
    key = jax.random.key(seed)
    keys = iter(jax.random.split(key, 40))
    f32 = jnp.float32

    def w(shape, fan_in):
        return jax.random.normal(next(keys), shape, f32) * (fan_in ** -0.5)

    def gain(shape):
        return 1.0 + 0.02 * jax.random.normal(next(keys), shape, f32)

    def small(shape, s):
        return s * jax.random.normal(next(keys), shape, f32)

    return {
        'x': jax.random.normal(next(keys), (BATCH, SEQ, D_MODEL), f32),
        'meta_tokens': small((N_META, D_MODEL), 1.0),
        'attn_norm': gain((DEPTH, D_MODEL)),
        'w_in': w((DEPTH, D_MODEL, IN_COLS), D_MODEL),
        'mla_cq_norm': gain((DEPTH, MLA_Q_LORA)),
        'w_mla_uq': w((DEPTH, MLA_Q_LORA, MLA_HEADS * MLA_QK), MLA_Q_LORA),
        'mla_ckv_norm': gain((DEPTH, MLA_KV_LORA)),
        'w_mla_ukv': w((DEPTH, MLA_KV_LORA, MLA_HEADS * (MLA_NOPE + MLA_V)), MLA_KV_LORA),
        'mla_q_norm': gain((DEPTH, MLA_QK)),
        'mla_k_norm': gain((DEPTH, MLA_QK)),
        'w_gla_g2': w((DEPTH, GLA_GATE_RANK, GLA_KW), GLA_GATE_RANK),
        'b_gla_g': small((DEPTH, GLA_KW), 0.1),
        'gla_o_norm': gain((DEPTH, GLA_DV)),
        'hgrn_lower_bounds': small((DEPTH, HGRN_KW), 0.1),
        'hgrn_o_norm': gain((DEPTH, HGRN_DV)),
        'w_mla_o': w((DEPTH, MLA_VW, D_MODEL), MLA_VW),
        'w_gla_o': w((DEPTH, GLA_VW, D_MODEL), GLA_VW),
        'w_hgrn_o': w((DEPTH, HGRN_VW, D_MODEL), HGRN_VW),
        'w_out': w((DEPTH, D_MODEL, D_MODEL), D_MODEL),
        'ffn_norm': gain((DEPTH, D_MODEL)),
        'w_ff_gate': w((N_DENSE, D_MODEL, D_FF), D_MODEL),
        'w_ff_up': w((N_DENSE, D_MODEL, D_FF), D_MODEL),
        'w_ff_down': w((N_DENSE, D_FF, D_MODEL), D_FF),
        'w_router': w((N_MOE, D_MODEL, N_EXPERTS), D_MODEL),
        'b_router': small((N_MOE, N_EXPERTS), 0.01),
        'w_exp_gate': w((N_MOE, N_EXPERTS, D_MODEL, D_EXPERT), D_MODEL),
        'w_exp_up': w((N_MOE, N_EXPERTS, D_MODEL, D_EXPERT), D_MODEL),
        'w_exp_down': w((N_MOE, N_EXPERTS, D_EXPERT, D_MODEL), D_EXPERT),
    }

def reference(x, meta_tokens, attn_norm, w_in, mla_cq_norm, w_mla_uq, mla_ckv_norm, w_mla_ukv, mla_q_norm, mla_k_norm,
              w_gla_g2, b_gla_g, gla_o_norm, hgrn_lower_bounds, hgrn_o_norm, w_mla_o, w_gla_o, w_hgrn_o, w_out,
              ffn_norm, w_ff_gate, w_ff_up, w_ff_down, w_router, b_router, w_exp_gate, w_exp_up, w_exp_down):
    B = x.shape[0]
    meta = jnp.broadcast_to(meta_tokens[None].astype(x.dtype), (B, N_META, D_MODEL))
    h = jnp.concatenate([meta, x], axis=1)
    L = h.shape[1]
    lbs = jax.nn.softmax(hgrn_lower_bounds.astype(jnp.float32), axis=0)
    lbs = jnp.cumsum(lbs, axis=0) - lbs[0]
    offsets = np.cumsum(IN_SPLITS)[:-1]
    for layer in range(DEPTH):
        u = rmsnorm(h, attn_norm[layer])
        (mla_dq, mla_dkv, mla_kr, gla_q, gla_k, gla_v, gla_gd, gla_r,
         hgrn_q, hgrn_f, hgrn_i, hgrn_g, gate_logits) = jnp.split(u @ w_in[layer], offsets, axis=-1)
        o_mla = mla_branch(mla_dq, mla_dkv, mla_kr, mla_cq_norm[layer], w_mla_uq[layer], mla_ckv_norm[layer],
                           w_mla_ukv[layer], mla_q_norm[layer], mla_k_norm[layer])
        o_gla = gla_branch(gla_q, gla_k, gla_v, gla_gd, gla_r, w_gla_g2[layer], b_gla_g[layer], gla_o_norm[layer])
        o_hgrn = hgrn2_branch(hgrn_q, hgrn_f, hgrn_i, hgrn_g, lbs[layer], hgrn_o_norm[layer])
        gates = jax.nn.sigmoid(gate_logits).reshape(B, L, N_BRANCH, D_MODEL)
        mixed = (gates[:, :, 0] * (o_mla @ w_mla_o[layer])
                 + gates[:, :, 1] * (o_gla @ w_gla_o[layer])
                 + gates[:, :, 2] * (o_hgrn @ w_hgrn_o[layer]))
        h = h + mixed @ w_out[layer]
        u = rmsnorm(h, ffn_norm[layer])
        if layer % 2 == 0:
            i = layer // 2
            h = h + swiglu(u, w_ff_gate[i], w_ff_up[i], w_ff_down[i])
        else:
            i = layer // 2
            h = h + moe_swiglu(u, w_router[i], b_router[i], w_exp_gate[i], w_exp_up[i], w_exp_down[i])
    return h[:, N_META:]


_drawn_inputs = setup_inputs


def setup_inputs(seed=0):
    import zlib

    import numpy as np

    out = dict(_drawn_inputs(seed))
    spreads = {}
    factors = {'mla_cq_norm': 8.0,
     'mla_ckv_norm': 4.665,
     'mla_q_norm': 6.479,
     'mla_k_norm': 8.0,
     'hgrn_lower_bounds': 16.973,
     'hgrn_o_norm': 3.103,
     'gla_o_norm': 3.77,
     'b_router': 23.187}
    for name, (base, spread) in spreads.items():
        noise = np.random.default_rng([zlib.crc32(name.encode()), seed]).standard_normal(out[name].shape)
        drawn = base * np.exp(spread * noise) if base else spread * noise
        out[name] = jnp.asarray(drawn.astype(out[name].dtype))
    for name, factor in factors.items():
        out[name] = (out[name] * factor).astype(out[name].dtype)
    return out
```

```python
from contextlib import ExitStack

import concourse.bass as bass
import numpy as np
from concourse import mybir

F32, F32R, I32 = mybir.dt.float32, mybir.dt.float32r, mybir.dt.int32
ALU = mybir.AluOpType
ACT = mybir.ActivationFunctionType
AX = mybir.AxisListType

P = 128
D = 1024
KD = D // P
META = 16
SEQ = 256
T = META + SEQ
DEPTH = 2
EPS = 1e-6
NEG = -1e30

HEADS, NOPE, ROPE, VDIM = 8, 64, 32, 64
QK = NOPE + ROPE
CH = 64
NCH = 5
LP = NCH * CH
OFF = CH - META
GLA_DK = 64
FF = 2816
NF = FF // P
NE = 8
DE = 3584
COL = dict(dq=0, dkv=256, kr=384 - 64, gq=416, gk=672, gv=928, gd=1440, r=1456,
           hq=1968, hf=2480, hi=2992, hg=3504, gate=4016)
BLOCKS = ((0, META), (META, P), (META + P, P))

RAW, SPLIT = 4, 3
MRAW, MSPLIT = 6, 3
EC = 256
N_GU = DE // EC
N_DN = DE // P // 2
ITEM = 2 * N_GU + N_DN
COMBINE_AT, TURN_AT, GATHER_AT = 5, 9, 32
OWN = 9

PCOL = {}


def param_columns():
    at = 0
    for name, n in (("attn", 8), ("ffn", 8), ("cq", 2), ("ckv", 1), ("qn", 1), ("kn", 1), ("bg", 2),
                    ("glao", 1), ("hgrno", 1), ("lb", 4)):
        PCOL[name] = at
        at += n
    return at


NPAR = param_columns()


def chunk_cols(c):
    if c == 0:
        return slice(OFF, CH), slice(0, META)
    return slice(c * CH, (c + 1) * CH), slice(META + (c - 1) * CH, META + c * CH)


def layer_jobs(layer):
    jobs = [("dq", 0), ("dq", 1), ("dkv", 0), ("kr", 0), ("gd", 0), ("gq", 0), ("gq", 1), ("gk", 0), ("gk", 1)]
    jobs += [("v", t) for t in range(4)]
    jobs += [("gate", m) for m in range(8)]
    jobs += [("f", 0), ("f", 1), ("q", 0), ("q", 1), ("v", 4), ("v", 5)]
    jobs += [("wo", m) for m in range(4)] + [("gate", 8 + m) for m in range(8)]
    jobs += [("f", 2), ("f", 3), ("q", 2), ("q", 3), ("v", 6), ("v", 7)]
    jobs += [("r", t) for t in range(4)] + [("wo", 4 + m) for m in range(4)]
    jobs += [("gate", 16 + m) for m in range(8)] + [("hg", t) for t in range(4)]
    jobs += [("wo", 8 + m) for m in range(4)] + [("wout", m) for m in range(8)]
    return [(layer, k, i) for k, i in jobs]


def ff_jobs(layer):
    jobs = []
    for f in range(NF):
        jobs += [("fg", f), ("fu", f)]
    jobs += [("fd", 3 * m + j) for m in range(8) for j in range(3)]
    return [(layer, k, i) for k, i in jobs]


def mla_steps(layer):
    out = [("ss", 0), ("vm", 0)]
    for h in range(0, HEADS, 2):
        for s in ("qk", "nrm", "rot", "sc", "pt", "pv"):
            out += [(s, h), (s, h + 1)]
    return [(layer, s, i) for s, i in out + [("ot", t) for t in range(4)]]


def la_steps(layer, unit):
    nh = 4 if unit == 0 else 2
    out = [("gz" if unit == 0 else "pre", 0), ("vt", 0), ("scan", 0), ("vt", 1), ("mul1", 0), ("vt", 2),
           ("mul2", 0), ("vt", 3), ("mul3", 0), ("vt", 4), ("kt", 0), ("kt", 1), ("ds", 0), ("ds", 1)]
    for h in range(0, nh, 2):
        for s in ("a", "o", "n"):
            out += [(s, h), (s, h + 1)]
    return [(3 * layer + unit, s, i) for s, i in out]


def build_schedule():
    jobs = []
    side = {}
    for layer in range(DEPTH):
        g0 = len(jobs)
        lj = layer_jobs(layer)
        kinds = [(k, i) for _, k, i in lj]
        jobs += lj
        mla = mla_steps(layer)
        gla = la_steps(layer, 0)
        at = 2 * (g0 + kinds.index(("kr", 0))) + 2
        end = 2 * (g0 + kinds.index(("wo", 0))) - 1
        for s in mla:
            side.setdefault(min(at, end), []).append(s)
            at += 1
        for steps, first, last in ((gla, ("v", 3), ("f", 0)), (la_steps(layer, 1), ("v", 5), ("f", 2)),
                                   (la_steps(layer, 2), ("v", 7), ("hg", 2))):
            at = 2 * (g0 + kinds.index(first)) + 2
            end = 2 * (g0 + kinds.index(last)) - 1
            for s in steps:
                side.setdefault(min(at, end), []).append(s)
                if s[1] not in ("scan", "mul1", "mul2", "mul3"):
                    at += 1
        if layer % 2 == 0:
            jobs += ff_jobs(layer)
    return jobs, side


def bass_hybrid_trunk(nc, A, out):
    jobs, side = build_schedule()
    NG = len(jobs)

    parts, outputs, of_job = 0, 0, []
    nexp, nsilu = 0, 0
    for layer, kind, i in jobs:
        n = 2 if kind == "wo" else 1
        j = dict(part=parts, parts=n, out=outputs, exp=nexp, silu=nsilu)
        parts += n
        outputs += n if kind != "fd" else int(i % 3 == 2)
        nexp += kind in ("q", "r", "hg", "fg")
        nsilu += kind in ("r", "hg", "fu")
        of_job.append(j)
    place = {job: g for g, job in enumerate(jobs)}

    def J(layer, kind, i):
        return of_job[place[(layer, kind, i)]]

    PE_PART = {"ss", "vm", "qk", "nrm", "rot", "sc", "pt", "pv", "ot", "gz", "vt", "kt", "ds", "a", "o", "n"}
    ACT_PART = {"ss", "vm", "qk", "nrm", "sc", "pt", "ot", "gz", "pre", "scan", "mul1", "mul2", "vt", "o", "n"}
    DVE_PART = {"ss", "qk", "nrm", "rot", "sc", "pt", "pv", "ot", "gz", "scan", "mul1", "mul2", "mul3", "kt",
                "ds", "a", "n"}
    number = {}
    count = dict(mla=[0, 0, 0], la=[0, 0, 0])
    MLA_NAMES = {"ss", "vm", "qk", "nrm", "rot", "sc", "pt", "pv", "ot"}
    for slot in sorted(side):
        for s in side[slot]:
            c = count["mla" if s[1] in MLA_NAMES else "la"]
            for e, have in enumerate((PE_PART, ACT_PART, DVE_PART)):
                c[e] += s[1] in have
            number[s] = tuple(c)

    def N(where, name, i, engine):
        return number[(where, name, i)][("pe", "act", "dve").index(engine)]

    def heads_of(unit):
        return 4 if unit % 3 == 0 else 2

    with ExitStack() as ctx:
        def sb(name, shape, dt=F32, c=ctx):
            return c.enter_context(nc.sbuf_tensor(name, shape, dt))

        def sem(name):
            return ctx.enter_context(nc.semaphore(name))

        bank = [ctx.enter_context(nc.psum_tensor(f"bank{i}", [P, 512], F32)) for i in range(8)]

        hT = sb("hT", [P, KD, T])
        mixed = sb("mixed", [P, KD, T])
        gt = sb("gt", [P, KD, T])
        rr = sb("rr", [P, T])
        C = sb("C", [P, A["consts"].shape[1]])
        par = sb("par", [P, DEPTH, NPAR])
        lbp = sb("lbp", [P, DEPTH, 2, 4])
        lbt = sb("lbt", [P, 4, 4])
        eps = sb("eps", [P, 1])
        cc = {}
        at = 0
        for name, n in CONSTS:
            cc[name] = slice(at, at + n)
            at += n
        ident, ones = C[:, cc["ident"]], C[:, cc["ones"]]

        mix = ExitStack()
        raw = [sb(f"raw{i}", [P, 1024], c=mix) for i in range(RAW)]
        hi = [sb(f"hi{i}", [P, 1024], F32R, mix) for i in range(SPLIT)]
        lo = [sb(f"lo{i}", [P, 1024], F32R, mix) for i in range(SPLIT)]
        UH = sb("UH", [P, KD, T], F32R, mix)
        UL = sb("UL", [P, KD, T], F32R, mix)
        ez = sb("ez", [P, 2, T], c=mix)

        tok = ExitStack()
        OH = sb("OH", [P, 4, T], F32R, tok)
        OL = sb("OL", [P, 4, T], F32R, tok)
        Q, K, G, B, X, QE, KE = (sb(n, [P, 2, LP], c=tok) for n in ("Q", "K", "G", "B", "X", "QE", "KE"))
        dec = sb("dec", [P, 2, NCH], c=tok)
        gdT = sb("gdT", [16, T], c=tok)
        wg2 = sb("wg2", [16, 256], c=tok)
        VT = sb("VT", [P, 4, T], c=tok)
        V = sb("V", [CH, NCH, 512], c=tok)
        KLT = sb("KLT", [CH, 4, 256], c=tok)
        S = sb("S", [P, 4, 4, P], c=tok)
        AT = sb("AT", [CH, 2, T], c=tok)
        ob = sb("ob", [P, 2, T], c=tok)
        osq = sb("osq", [P, 2, T], c=tok)
        rl = sb("rl", [P, 2, T], c=tok)
        O = sb("O", [P, 2, 4, T], c=tok)
        dqT = sb("dqT", [P, 3, T], c=tok)
        rin = gt[:, 3:5, :]
        wuq = sb("wuq", [P, 2, HEADS * QK], c=tok)
        wukv = sb("wukv", [P, HEADS * (NOPE + VDIM)], c=tok)
        vtok = sb("vtok", [P, 3, 512], c=tok)
        qk = sb("qk", [QK, 2, 2, T], c=tok)
        kr_keep = sb("kr_keep", [QK, T], c=tok)
        qsq = sb("qsq", [QK, 2, 2, T], c=tok)
        pr = sb("pr", [P, 2, 432], c=tok)
        mx = sb("mx", [P, 2, 3], c=tok)
        sm = sb("sm", [P, 2, 3], c=tok)
        ptf = sb("ptf", [P, 2, 384], c=tok)
        ptm = sb("ptm", [META, 2, T], c=tok)
        otok = sb("otok", [P, 3, 512], c=tok)
        tok.close()
        dense = ExitStack()
        HH = sb("HH", [P, NF, T], F32R, dense)
        HL = sb("HL", [P, NF, T], F32R, dense)
        dense.close()
        mix.close()

        mraw = [sb(f"mraw{i}", [P, 2048]) for i in range(MRAW)]
        mhi = [sb(f"mhi{i}", [P, 2048], F32R) for i in range(MSPLIT)]
        mlo = [sb(f"mlo{i}", [P, 2048], F32R) for i in range(MSPLIT)]
        utok = sb("utok", [P, 2, D])
        acc = sb("acc", [P, 2, D])
        xh = sb("xh", [P, KD, P], F32R)
        xl = sb("xl", [P, KD, P], F32R)
        sg = sb("sg", [P, 2, EC])
        hs = sb("hs", [P, 2, EC])
        hh = sb("hh", [P, DE // P, P], F32R)
        hl = sb("hl", [P, DE // P, P], F32R)
        ys = sb("ys", [P, D])
        sel = sb("sel", [P, 2, P])
        selw = sb("selw", [P, 2, P])
        selT = sb("selT", [P, 2, P])
        MC = sb("MC", [P, P * 3])
        iota, tri = MC[:, 0:P], MC[:, P:2 * P]
        wr = sb("wr", [P, KD, NE])
        brb = sb("brb", [P, NE])
        rt = sb("rt", [P, 14, 2, NE])
        slot, top, w12 = sb("slot", [P, 2, 2]), sb("top", [P, 2, 4]), sb("w12", [P, 2, 2])
        oh, ow = sb("oh", [P, 2, P]), sb("ow", [P, 2, P])
        iit = sb("iit", [1, 1, 16])
        it_i = sb("it_i", [1, 16], I32)
        nit_i = sb("nit_i", [1, 1], I32)

        landed = [sem(f"landed{i}") for i in range(RAW)]
        const_landed, par_landed, x_landed, small_landed = (
            sem("const_landed"), sem("par_landed"), sem("x_landed"), sem("small_landed"))
        small_used = sem("small_used")
        zeroed = sem("zeroed")
        hi_made, lo_made = sem("hi_made"), sem("lo_made")
        stream_done = sem("stream_done")
        bank_free = [sem("bank0_free"), sem("bank1_free")]
        x_turned, h_loaded = sem("x_turned"), sem("h_loaded")
        norm_sq, norm_sum, norm_r, u_ready = sem("norm_sq"), sem("norm_sum"), sem("norm_r"), sem("u_ready")
        exp_made, silu_done = sem("exp_made"), sem("silu_done")
        mix_done = sem("mix_done")
        f_ready, lb_exp, lb_sub, lb_ready = sem("f_ready"), sem("lb_exp"), sem("lb_sub"), sem("lb_ready")
        mla_psum, mla_act, mla_dve = sem("mla_psum"), sem("mla_act"), sem("mla_dve")
        la_psum, la_act, la_dve = sem("la_psum"), sem("la_act"), sem("la_dve")
        act_step, dve_step = sem("act_step"), sem("dve_step")
        mlanded = [sem(f"mlanded{i}") for i in range(MRAW)]
        moe_const, turned_u, turned_h = sem("moe_const"), sem("turned_u"), sem("turned_h")
        u_whole = sem("u_whole")
        utok_made, acc_loaded = sem("utok_made"), sem("acc_loaded")
        logits_ready, router_diff, router_exp = sem("logits_ready"), sem("router_diff"), sem("router_exp")
        chosen, ranked, items_ready = sem("chosen"), sem("ranked"), sem("items_ready")
        sel_ready, sel_turned, selT_ready = sem("sel_ready"), sem("sel_turned"), sem("selT_ready")
        x_gathered, xh_made, xl_made = sem("x_gathered"), sem("xh_made"), sem("xl_made")
        mhi_made, mlo_made, chunk_done = sem("mhi_made"), sem("mlo_made"), sem("chunk_done")
        sg_made, h_made, h_turned, hh_made, hl_made = (
            sem("sg_made"), sem("h_made"), sem("h_turned"), sem("hh_made"), sem("hl_made"))
        y_out, combined, acc_added, item_step = sem("y_out"), sem("combined"), sem("acc_added"), sem("item_step")
        out_stored = sem("out_stored")

        class Steps:

            def __init__(self, eng, s):
                self.eng, self.s, self.n = eng, s, 0

            def __call__(self, ins):
                ins.then_inc(self.s, 1)
                self.n += 1

            def wait(self):
                self.eng.wait_ge(self.s, self.n)

        def drained(eng, o):
            eng.wait_ge(bank_free[o % 2], o // 2 + 1)

        def tile_source(layer, kind, i):
            w = A["w_in"][layer].rearrange("(k p) c -> p k c", p=P)
            if kind in ("dq", "dkv", "kr", "gd", "gq", "gk", "r", "hg", "gate"):
                c0 = COL[kind] + (i * P if kind not in ("kr", "gd") else 0)
                return w[:, :, c0:c0 + P], (KD, P)
            if kind == "v":
                c0 = COL["gv"] + i * P if i < 4 else COL["hi"] + (i - 4) * P
                return w[:, :, c0:c0 + P], (KD, P)
            if kind in ("f", "q"):
                c0 = COL["hf" if kind == "f" else "hq"] + i * P
                return w[:, :, c0:c0 + P], (KD, P)
            if kind == "wo":
                wo = A[("w_mla_o", "w_gla_o", "w_hgrn_o")[i // 4]][layer].rearrange("(k p) c -> p k c", p=P)
                return wo[:, :, (i % 4) * 256:(i % 4 + 1) * 256], (4, 256)
            if kind == "wout":
                wo = A["w_out"][layer].rearrange("(k p) c -> p k c", p=P)
                return wo[:, :, i * P:(i + 1) * P], (KD, P)
            if kind in ("fg", "fu"):
                wf = A["w_ff_gate" if kind == "fg" else "w_ff_up"][layer // 2].rearrange("(k p) c -> p k c", p=P)
                return wf[:, :, i * P:(i + 1) * P], (KD, P)
            m, j = i // 3, i % 3
            wf = A["w_ff_down"][layer // 2].rearrange("(k p) c -> p k c", p=P)
            n = min(8, NF - 8 * j)
            return wf[:, 8 * j:8 * j + n, m * P:(m + 1) * P], (n, P)

        def expert_chunk(e, k):
            if k < 2 * N_GU:
                w = A["w_exp_gate" if k % 2 == 0 else "w_exp_up"]
                w = w.rearrange("l e (k p) c -> (l e) p k c", p=P)
                j = k // 2
                return w[bass.ds(e, 1), :, :, j * EC:(j + 1) * EC].rearrange("o p k c -> (o p) k c"), (KD, EC)
            w = A["w_exp_down"].rearrange("l e (k p) c -> (l e) p k c", p=P)
            j = k - 2 * N_GU
            return w[bass.ds(e, 1), :, 2 * j:2 * j + 2, :].rearrange("o p k c -> (o p) k c"), (2, D)

        last_out = of_job[-1]["out"]
        norm_before = {g for g, (_, k, i) in enumerate(jobs) if g and i == 0 and k in ("dq", "fg")}
        norm_after = {n + 1: of_job[g]["out"] - 1 for n, g in enumerate(sorted(norm_before))}
        norm_after[len(norm_before) + 1] = last_out
        need_u = {g: n for n, g in enumerate(g for g, (_, k, i) in enumerate(jobs)
                                             if i == 0 and k in ("dq", "wout", "fg"))}
        block = ctx.enter_context(nc.Block())

        @block.sync
        def _(sp):
            sp.dma_start(gt[:, :, :].rearrange("p k t -> p (k t)")[:, 0:2 * D].rearrange("p (b d) -> p b d", b=2),
                         A["x"][0].rearrange("(b p) d -> p b d", p=P)).then_inc(x_landed, 16)
            sp.dma_start(mixed[:, :, :].rearrange("p k t -> p (k t)")[0:META, 0:D],
                         A["meta_tokens"]).then_inc(x_landed, 16)
            sp.dma_start(C[:], A["consts"]).then_inc(const_landed, 16)
            sp.dma_start(par[:], A["params"]).then_inc(par_landed, 16)
            for g, (layer, kind, i) in enumerate(jobs):
                if kind == "gd":
                    if layer:
                        drained(sp, J(layer, "dq", 0)["out"] - 1)
                        drained(sp, J(layer, "dq", 0)["out"] - 2)
                    sp.dma_start(wuq[:], A["w_mla_uq"][layer].rearrange("(k p) c -> p k c", p=P)).then_inc(small_landed, 16)
                    sp.dma_start(wukv[:], A["w_mla_ukv"][layer]).then_inc(small_landed, 16)
                    sp.dma_start(wg2[:], A["w_gla_g2"][layer]).then_inc(small_landed, 16)
                if g >= RAW:
                    sp.wait_ge(lo_made, g - RAW + 1)
                src, (r, c) = tile_source(layer, kind, i)
                sp.dma_start(raw[g % RAW][:, 0:r * c].rearrange("p (r c) -> p r c", r=r), src).then_inc(landed[g % RAW], 16)
            drained(sp, last_out)
            drained(sp, last_out - 1)
            sp.dma_start(MC[:], A["moe_consts"]).then_inc(moe_const, 16)
            sp.dma_start(wr[:], A["w_router"][0].rearrange("(k p) e -> p k e", p=P)).then_inc(moe_const, 16)
            sp.dma_start(brb[:], A["b_router"][0:1, :].broadcast_to([P, NE])).then_inc(moe_const, 16)
            sp.wait_ge(items_ready, 2)
            n_items = sp.value_load(nit_i[0:1, 0:1], min_val=1, max_val=12)
            with sp.Fori(0, n_items) as i:
                e = sp.value_load(it_i[0:1, bass.ds(i, 1)], min_val=0, max_val=NE - 1)
                for k in range(ITEM):
                    sp.wait_ge(mlo_made, i * ITEM + (k + 1))
                    src, (r, c) = expert_chunk(e, k)
                    sp.dma_start(mraw[k % MRAW][:].rearrange("p (r c) -> p r c", r=r), src).then_inc(mlanded[k % MRAW], 16)
            for k in range(MSPLIT):
                sp.wait_ge(mlo_made, n_items * ITEM + (k + 1))
                sp.dma_start(mraw[k % MRAW][:, 0:NE], A["moe_consts"][:, 0:NE]).then_inc(mlanded[k % MRAW], 16)
            sp.wait_ge(acc_added, n_items * 4 + 4)
            sp.dma_start(out[0].rearrange("(b p) d -> p b d", p=P), acc[:]).then_inc(out_stored, 16)
            sp.wait_ge(out_stored, 16)

        @block.scalar
        def _(act):
            st = Steps(act, act_step)
            A_ = nc.scalar.activation

            def split_hi(g):
                layer, kind, i = jobs[g]
                n = tile_source(layer, kind, i)[1]
                n = n[0] * n[1]
                act.wait_ge(landed[g % RAW], 16 * (g // RAW + 1))
                if g >= SPLIT:
                    act.wait_ge(stream_done, of_job[g - SPLIT]["part"] + of_job[g - SPLIT]["parts"])
                A_(hi[g % SPLIT][:, 0:n], raw[g % RAW][:, 0:n], ACT.Copy).then_inc(hi_made, 1)

            def norm(phase):
                if phase == 0:
                    act.wait_ge(h_loaded, 8)
                else:
                    drained(act, norm_after[phase])
                    drained(act, norm_after[phase] - 1)
                A_(gt[:], hT[:], ACT.Square).then_inc(norm_sq, 1)
                act.wait_ge(norm_sum, phase + 1)
                st(A_(rr[:], bank[2][:, 0:T], ACT.Ln, bias=eps[:, 0:1], scale=1.0 / D))
                st.wait()
                A_(rr[:], rr[:], ACT.Exp, scale=-0.5).then_inc(norm_r, 1)

            def evacuate(g):
                layer, kind, i = jobs[g]
                j = of_job[g]
                o = j["out"]
                if kind in ("gk", "wo", "wout", "fd", "fu"):
                    return
                ps = bank[o % 2][:, 0:T]
                free = bank_free[o % 2]
                act.wait_ge(stream_done, j["part"] + 1)
                if kind in ("dq", "dkv"):
                    t = i if kind == "dq" else 2
                    st(A_(dqT[:, t, :], ps, ACT.Copy))
                    A_(gt[:, t, :], ps, ACT.Square).then_inc(free, 1)
                elif kind == "kr":
                    st(A_(qk[NOPE:QK, 0, 1, :], ps[NOPE:QK], ACT.Copy))
                    A_(qk[NOPE:QK, 1, 1, :], ps[NOPE:QK], ACT.Copy).then_inc(free, 1)
                elif kind == "gq":
                    A_(Q[:, i, OFF:LP], ps, ACT.Copy, scale=GLA_DK ** -0.5).then_inc(free, 1)
                elif kind == "gd":
                    A_(gdT[:], ps[0:16], ACT.Copy).then_inc(free, 1)
                elif kind == "v":
                    A_(VT[:, i if i < 4 else (i - 4) % 2, :], ps, ACT.Copy).then_inc(free, 1)
                elif kind == "f":
                    A_(X[:, i % 2, OFF:LP], ps, ACT.Exp, scale=-1.0).then_inc(free, 1)
                elif kind == "q":
                    A_(QE[:, i % 2, OFF:LP], ps, ACT.Exp, scale=-1.0).then_inc(exp_made, 1)
                elif kind in ("r", "hg", "fg"):
                    if j["silu"] >= 2:
                        act.wait_ge(silu_done, j["silu"] - 1)
                    A_(ez[:, j["silu"] % 2, :], ps, ACT.Exp, scale=-1.0).then_inc(exp_made, 1)
                elif kind == "gate":
                    b, m = divmod(i, 8)
                    if b:
                        act.wait_ge(mix_done, 8 * (3 * layer + b - 1) + m + 1)
                    elif m < 5:
                        act.wait_ge(mla_dve, N(layer, "ss", 0, "dve"))
                    A_(gt[:, m, :], ps, ACT.Exp, scale=-1.0).then_inc(free, 1)

            def mla(layer, name, i):
                p = i % 2
                Ma, Mb = bank[2 + 2 * p], bank[3 + 2 * p]
                act.wait_ge(mla_psum, N(layer, name, i, "pe"))
                if name == "ss":
                    st(A_(rin[:, 0, :], bank[2][:, 0:T], ACT.Ln, bias=eps[:, 0:1], scale=1.0 / 256))
                    st(A_(rin[:, 1, :], bank[3][:, 0:T], ACT.Ln, bias=eps[:, 0:1], scale=1.0 / 128))
                    st.wait()
                    A_(rin, rin, ACT.Exp, scale=-0.5).then_inc(mla_act, 1)
                elif name == "vm":
                    st(A_(vtok[0:META, 0, :], bank[4][0:META, :], ACT.Copy))
                    st(A_(vtok[:, 1, :], bank[5][:], ACT.Copy))
                    A_(vtok[:, 2, :], bank[2][:], ACT.Copy).then_inc(mla_act, 1)
                elif name == "qk":
                    if i >= 2:
                        act.wait_ge(mla_psum, N(layer, "sc", i - 2, "pe"))
                    st(A_(qk[:, p, 0, :], Ma[0:QK, 0:T], ACT.Copy))
                    A_(qsq[:, p, 0, :], Ma[0:QK, 0:T], ACT.Square).then_inc(mla_act, 1)
                elif name == "nrm":
                    st(A_(qsq[:, p, 0, :], Ma[0:QK, 0:T], ACT.Ln, bias=eps[0:QK, 0:1], scale=1.0 / QK))
                    st(A_(qsq[:, p, 1, :], Mb[0:QK, 0:T], ACT.Ln, bias=eps[0:QK, 0:1], scale=1.0 / QK))
                    st.wait()
                    A_(qsq[:, p, :, :], qsq[:, p, :, :], ACT.Exp, scale=-0.5).then_inc(mla_act, 1)
                elif name == "sc":
                    act.wait_ge(mla_dve, N(layer, "sc", i, "dve"))
                    st(A_(pr[:, p, 0:272], pr[:, p, 0:272], ACT.Exp, bias=mx[:, p, 0:1], accum_out=sm[:, p, 0:1]))
                    st(A_(pr[:, p, 272:416], pr[:, p, 272:416], ACT.Exp, bias=mx[:, p, 1:2], accum_out=sm[:, p, 1:2]))
                    A_(pr[0:META, p, 416:432], pr[0:META, p, 416:432], ACT.Exp, bias=mx[0:META, p, 2:3],
                       accum_out=sm[0:META, p, 2:3]).then_inc(mla_act, 1)
                elif name == "pt":
                    A_(ptf[:, p, :], Mb[:, 0:384], ACT.Copy).then_inc(mla_act, 1)
                elif name == "ot":
                    if layer:
                        act.wait_ge(stream_done, J(layer - 1, "wo", 11)["part"] + 2)
                    A_(OH[:, i, :], bank[2 + i][:, 0:T], ACT.Copy).then_inc(mla_act, 1)

            def la(unit, name, i):
                scale = 1.0 / 16 if unit % 3 == 0 else 1.0
                layer = unit // 3
                L = bank[6 + i % 2]
                if name == "gz":
                    act.wait_ge(la_psum, N(unit, name, i, "pe"))
                    for t in range(2):
                        st(A_(X[:, t, OFF:LP], bank[6 + t][:, 0:T], ACT.Abs,
                              bias=par[:, layer, PCOL["bg"] + t:PCOL["bg"] + t + 1]))
                    st.wait()
                    st(A_(X[:, :, OFF:LP], X[:, :, OFF:LP], ACT.Exp, scale=-1.0))
                    st.wait()
                    A_(X[:, :, OFF:LP], X[:, :, OFF:LP], ACT.Ln, bias=1.0).then_inc(la_act, 1)
                elif name == "pre":
                    act.wait_ge(f_ready, 4 * layer + 2 * (unit % 3))
                    A_(G[:, :, OFF:LP], X[:, :, OFF:LP], ACT.Ln).then_inc(la_act, 1)
                elif name == "scan":
                    act.wait_ge(la_dve, N(unit, "scan", 0, "dve"))
                    st(A_(QE[:], X[:], ACT.Exp, scale=scale))
                    A_(KE[:], X[:], ACT.Exp, scale=-scale).then_inc(la_act, 1)
                elif name == "mul1":
                    act.wait_ge(la_act, N(unit, "scan", 0, "act"))
                    A_(X[:], B[:], ACT.Exp, scale=scale).then_inc(la_act, 1)
                elif name == "mul2":
                    act.wait_ge(la_dve, N(unit, "mul2", 0, "dve"))
                    st(A_(dec[:], B[:].rearrange("p t (c j) -> p t c j", j=CH)[:, :, :, CH - 1], ACT.Exp, scale=scale))
                    A_(X[:], X[:], ACT.Exp, scale=scale).then_inc(la_act, 1)
                elif name == "vt":
                    act.wait_ge(la_psum, N(unit, name, i, "pe"))
                    rows, w = (META if i == 0 else CH), heads_of(unit) * P
                    A_(V[0:rows, i, 0:w], L[0:rows, 0:w], ACT.Copy).then_inc(la_act, 1)
                elif name == "o":
                    act.wait_ge(la_psum, N(unit, name, i, "pe"))
                    if (unit, i) != (0, 0) and (unit, i) != (0, 1):
                        before = (unit, "n", i - 2) if i >= 2 else (unit - 1, "n", heads_of(unit - 1) - 2 + i)
                        act.wait_ge(la_dve, N(*before, "dve"))
                    st(A_(ob[:, i % 2, :], L[:, 0:T], ACT.Copy))
                    A_(osq[:, i % 2, :], L[:, 0:T], ACT.Square).then_inc(la_act, 1)
                elif name == "n":
                    act.wait_ge(la_psum, N(unit, name, i, "pe"))
                    st(A_(rl[:, i % 2, :], L[:, 0:T], ACT.Ln, bias=eps[:, 0:1], scale=1.0 / P))
                    st.wait()
                    A_(rl[:, i % 2, :], rl[:, i % 2, :], ACT.Exp, scale=-0.5).then_inc(la_act, 1)

            act.wait_ge(lb_sub, 1)
            A_(lbt[:, 1:3, :], lbt[:, 1:3, :], ACT.Exp).then_inc(lb_exp, 1)
            for g in range(2):
                split_hi(g)
            norm(0)
            phase = 1
            for g in range(NG):
                if g + 2 < NG:
                    split_hi(g + 2)
                if g in norm_before:
                    norm(phase)
                    phase += 1
                for half in range(2):
                    if half == 1:
                        evacuate(g)
                    for s in side.get(2 * g + half, ()):
                        if s[1] in ACT_PART:
                            (mla if s[1] in MLA_NAMES else la)(*s)

            norm(phase)
            for b in range(2):
                for half in range(2):
                    act.wait_ge(turned_u, 2 * b + half + 1)
                    A_(utok[:, b, half * 512:(half + 1) * 512], bank[half][:], ACT.Copy).then_inc(utok_made, 1)
            act.wait_ge(router_diff, 1)
            A_(top[:, :, 2], top[:, :, 2], ACT.Exp).then_inc(router_exp, 1)
            act.wait_ge(items_ready, 2)
            n_items = act.value_load(nit_i[0:1, 0:1], min_val=1, max_val=12)

            def expert_hi(k, landings):
                act.wait_ge(mlanded[k % MRAW], landings)
                A_(mhi[k % MSPLIT][:], mraw[k % MRAW][:], ACT.Copy).then_inc(mhi_made, 1)

            def gathered_hi(first):
                for half in range(2):
                    act.wait_ge(x_gathered, first + half)
                    A_(xh[:, 4 * half:4 * half + 4, :].rearrange("p k s -> p (k s)"), bank[4 + half][:],
                       ACT.Copy).then_inc(xh_made, 1)

            act.sem_inc(y_out, 2)
            for k in range(MSPLIT):
                expert_hi(k, 16)
            gathered_hi(1)
            with act.Fori(0, n_items) as i:
                for k in range(ITEM):
                    act.wait_ge(chunk_done, i * ITEM + (k + 1))
                    if k % 2 == 1 and k < 2 * N_GU:
                        j = k // 2
                        act.wait_ge(h_made, i * N_GU + (j + 1))
                        A_(sg[:, j % 2, :], bank[j % 2][:, 0:EC], ACT.Silu).then_inc(sg_made, 1)
                    n = k + MSPLIT
                    expert_hi(n % ITEM, (i * (ITEM // MRAW) + (n // MRAW + 1)) * 16)
                    if k % 2 == 0 and 4 <= k <= 2 * N_GU + 2:
                        j = (k - 4) // 2
                        act.wait_ge(h_turned, i * N_GU + (j + 1))
                        A_(hh[:, 2 * j:2 * j + 2, :].rearrange("p f s -> p (f s)"), bank[6 + j % 2][:, 0:2 * P],
                           ACT.Copy).then_inc(hh_made, 1)
                    if k == GATHER_AT + 1:
                        gathered_hi(i * 2 + 3)
                for half in range(2):
                    A_(ys[:, half * 512:(half + 1) * 512], bank[2 + half][:], ACT.Copy).then_inc(y_out, 1)

        @block.vector
        def _(dve):
            st = Steps(dve, dve_step)
            E = nc.vector
            TT, TS, STT, CP = E.tensor_tensor, E.tensor_scalar, E.scalar_tensor_tensor, E.tensor_copy

            def split_lo(g):
                layer, kind, i = jobs[g]
                n = tile_source(layer, kind, i)[1]
                n = n[0] * n[1]
                dve.wait_ge(hi_made, g + 1)
                TT(lo[g % SPLIT][:, 0:n], raw[g % RAW][:, 0:n], hi[g % SPLIT][:, 0:n].bitcast(F32),
                   ALU.subtract).then_inc(lo_made, 1)

            def norm(phase, gain, split):
                dve.wait_ge(norm_r, phase + 1)
                for k in range(KD + 2):
                    if k < KD:
                        st(STT(mixed[:, k, :], hT[:, k, :], gain[:, k:k + 1], rr[:], ALU.mult, ALU.mult))
                    if split and 1 <= k <= KD:
                        if k < KD:
                            dve.wait_ge(dve_step, st.n - 1 - (k >= 2))
                        else:
                            st.wait()
                        st(CP(UH[:, k - 1, :], mixed[:, k - 1, :]))
                    if split and k >= 2:
                        st.wait()
                        TT(UL[:, k - 2, :], mixed[:, k - 2, :], UH[:, k - 2, :].bitcast(F32),
                           ALU.subtract).then_inc(u_ready, 1)
                if not split:
                    st.wait()
                    E.memset(ys[:], 0.0).then_inc(u_whole, 1)

            def zero_pads():
                for t in (Q, K, G):
                    st(E.memset(t[:, :, 0:OFF], 0.0))
                st(E.memset(AT[:], 0.0))

            def sigmoid(x):
                st(TS(x, x, 1.0, None, ALU.add))
                st.wait()
                st(E.reciprocal(x, x))
                st.wait()

            def evacuate(g):
                layer, kind, i = jobs[g]
                j = of_job[g]
                o = j["out"]
                if kind in ("dq", "dkv", "kr", "gq", "gd", "v") or kind == "fd" and i % 3 < 2:
                    return
                ps = bank[o % 2][:, 0:T]
                free = bank_free[o % 2]
                if kind == "gk":
                    dve.wait_ge(stream_done, j["part"] + 1)
                    CP(K[:, i, OFF:LP], ps).then_inc(free, 1)
                elif kind == "f":
                    t = i % 2
                    drained(dve, o)
                    if layer == 0 and i == 0:
                        dve.wait_ge(lb_ready, 1)
                    x = X[:, t, OFF:LP]
                    sigmoid(x)
                    st(TS(x, x, lbp[:, layer, 1, i:i + 1], lbp[:, layer, 0, i:i + 1], ALU.mult, ALU.add))
                    st.wait()
                    TS(K[:, t, OFF:LP], x, -1.0, 1.0, ALU.mult, ALU.add).then_inc(f_ready, 1)
                elif kind == "q":
                    dve.wait_ge(exp_made, j["exp"] + 1)
                    x = QE[:, i % 2, OFF:LP]
                    sigmoid(x)
                    TT(Q[:, i % 2, OFF:LP], x, ps, ALU.mult).then_inc(free, 1)
                elif kind in ("r", "hg"):
                    dve.wait_ge(exp_made, j["exp"] + 1)
                    x = ez[:, j["silu"] % 2, :]
                    sigmoid(x)
                    TT(x, x, ps, ALU.mult).then_inc(free, 1)
                    drained(dve, o)
                    st(TT(x, x, O[:, 0 if kind == "r" else 1, i, :], ALU.mult))
                    st.wait()
                    if i == 0:
                        dve.wait_ge(stream_done, J(layer, "wo", 3 if kind == "r" else 7)["part"] + 2)
                    st(CP(OH[:, i, :], x))
                    st.wait()
                    TT(OL[:, i, :], x, OH[:, i, :].bitcast(F32), ALU.subtract).then_inc(silu_done, 1)
                elif kind == "gate":
                    drained(dve, o)
                    sigmoid(gt[:, i % 8, :])
                elif kind == "wo":
                    b = i // 4
                    for half in range(2):
                        m = 2 * (i % 4) + half
                        oo = o + half
                        dve.wait_ge(stream_done, j["part"] + half + 1)
                        x = gt[:, m, :]
                        TT(x, x, bank[oo % 2][:, 0:T], ALU.mult).then_inc(bank_free[oo % 2], 1)
                        drained(dve, oo)
                        if b == 0:
                            CP(mixed[:, m, :], x).then_inc(mix_done, 1)
                        else:
                            TT(mixed[:, m, :], mixed[:, m, :], x, ALU.add).then_inc(mix_done, 1)
                        if b == 2:
                            dve.wait_ge(mix_done, 24 * layer + 16 + m + 1)
                            st(CP(UH[:, m, :], mixed[:, m, :]))
                            st.wait()
                            TT(UL[:, m, :], mixed[:, m, :], UH[:, m, :].bitcast(F32),
                               ALU.subtract).then_inc(u_ready, 1)
                elif kind in ("wout", "fd"):
                    m = i if kind == "wout" else i // 3
                    dve.wait_ge(stream_done, j["part"] + 1)
                    TT(hT[:, m, :], hT[:, m, :], ps, ALU.add).then_inc(free, 1)
                elif kind == "fg":
                    dve.wait_ge(exp_made, j["exp"] + 1)
                    x = ez[:, j["silu"] % 2, :]
                    sigmoid(x)
                    TT(x, x, ps, ALU.mult).then_inc(free, 1)
                elif kind == "fu":
                    dve.wait_ge(stream_done, j["part"] + 1)
                    drained(dve, o - 1)
                    x = ez[:, j["silu"] % 2, :]
                    TT(x, x, ps, ALU.mult).then_inc(free, 1)
                    drained(dve, o)
                    st(CP(HH[:, i, :], x))
                    st.wait()
                    TT(HL[:, i, :], x, HH[:, i, :].bitcast(F32), ALU.subtract).then_inc(silu_done, 1)

            def mla(layer, name, i):
                p = i % 2
                Ma, Mb = bank[2 + 2 * p], bank[3 + 2 * p]
                gain = lambda n, rows=P: par[0:rows, layer, PCOL[n]:PCOL[n] + 1]
                if name == "ss":
                    dve.wait_ge(mla_act, N(layer, name, i, "act"))
                    for t in range(3):
                        g = par[:, layer, PCOL["cq"] + t:PCOL["cq"] + t + 1] if t < 2 else gain("ckv")
                        ins = STT(dqT[:, t, :], dqT[:, t, :], g, rin[:, t // 2, :], ALU.mult, ALU.mult)
                        if t < 2:
                            st(ins)
                        else:
                            ins.then_inc(mla_dve, 1)
                elif name == "qk":
                    dve.wait_ge(mla_psum, N(layer, name, i, "pe"))
                    if i >= 2:
                        dve.wait_ge(mla_act, N(layer, name, i, "act"))
                        st(CP(qk[NOPE:QK, p, 1, :], kr_keep[NOPE:QK, :]))
                    else:
                        st(CP(kr_keep[NOPE:QK, :], qk[NOPE:QK, p, 1, :]))
                    st(CP(qk[0:NOPE, p, 1, :], Mb[0:NOPE, 0:T]))
                    st.wait()
                    TT(qsq[:, p, 1, :], qk[:, p, 1, :], qk[:, p, 1, :], ALU.mult).then_inc(mla_dve, 1)
                elif name == "nrm":
                    dve.wait_ge(mla_act, N(layer, name, i, "act"))
                    st(STT(qk[:, p, 0, :], qk[:, p, 0, :], gain("qn", QK), qsq[:, p, 0, :], ALU.mult, ALU.mult))
                    STT(qk[:, p, 1, :], qk[:, p, 1, :], gain("kn", QK), qsq[:, p, 1, :],
                        ALU.mult, ALU.mult).then_inc(mla_dve, 1)
                elif name == "rot":
                    dve.wait_ge(mla_psum, N(layer, name, i, "pe"))
                    cos, sin = C[NOPE:QK, cc["cos"]], C[NOPE:QK, cc["sin"]]
                    for t, M in ((0, Ma), (1, Mb)):
                        st(TT(qsq[NOPE:QK, p, t, :], sin, M[NOPE:QK, 0:T], ALU.mult))
                        st(TT(qk[NOPE:QK, p, t, :], qk[NOPE:QK, p, t, :], cos, ALU.mult))
                    st.wait()
                    TT(qk[NOPE:QK, p, :, :], qk[NOPE:QK, p, :, :], qsq[NOPE:QK, p, :, :], ALU.add).then_inc(mla_dve, 1)
                elif name == "sc":
                    dve.wait_ge(mla_psum, N(layer, name, i, "pe"))
                    if (layer, i) not in ((0, 0), (0, 1)):
                        before = (layer, "pt", i - 2) if i >= 2 else (layer - 1, "pt", HEADS - 2 + i)
                        dve.wait_ge(mla_psum, N(*before, "pe"))
                    mask = C[:, cc["smask"]]
                    st(STT(pr[:, p, 0:416], Ma[:, 0:416], QK ** -0.5, mask[:, 0:416], ALU.mult, ALU.add))
                    st(STT(pr[0:META, p, 416:432], Ma[0:META, 416:432], QK ** -0.5, mask[0:META, 416:432],
                           ALU.mult, ALU.add))
                    st.wait()
                    st(E.tensor_reduce(mx[:, p, 0:1], pr[:, p, 0:272], AX.X, ALU.max, negate=True))
                    st(E.tensor_reduce(mx[:, p, 1:2], pr[:, p, 272:416], AX.X, ALU.max, negate=True))
                    E.tensor_reduce(mx[0:META, p, 2:3], pr[0:META, p, 416:432], AX.X, ALU.max,
                                    negate=True).then_inc(mla_dve, 1)
                elif name == "pt":
                    dve.wait_ge(mla_psum, N(layer, name, i, "pe"))
                    st(E.reciprocal(sm[:, p, 0:2], sm[:, p, 0:2]))
                    st(E.reciprocal(sm[0:META, p, 2:3], sm[0:META, p, 2:3]))
                    st(CP(ptm[:, p, 0:256], Ma[0:META, 0:256]))
                    CP(ptm[:, p, 256:272], Ma[0:META, 256:272]).then_inc(mla_dve, 1)
                elif name == "pv":
                    dve.wait_ge(mla_psum, N(layer, name, i, "pe"))
                    dve.wait_ge(mla_dve, N(layer, "pt", i, "dve"))
                    c = slice(i * VDIM, (i + 1) * VDIM)
                    st(TS(otok[:, 2, c], Ma[:, 0:VDIM], sm[:, p, 0:1], None, ALU.mult))
                    st(TS(otok[:, 1, c], Mb[:, 0:VDIM], sm[:, p, 1:2], None, ALU.mult))
                    TS(otok[0:META, 0, c], Mb[0:META, VDIM:2 * VDIM], sm[0:META, p, 2:3], None,
                       ALU.mult).then_inc(mla_dve, 1)
                elif name == "ot":
                    dve.wait_ge(mla_act, N(layer, name, i, "act"))
                    TT(OL[:, i, :], bank[2 + i][:, 0:T], OH[:, i, :].bitcast(F32), ALU.subtract).then_inc(mla_dve, 1)

            def la(unit, name, i):
                layer, u = divmod(unit, 3)
                L = bank[6 + i % 2]
                chunks = lambda t: t[:].rearrange("p t (c j) -> p (t c) j", j=CH)
                if name == "gz":
                    dve.wait_ge(la_act, N(unit, name, i, "act"))
                    for t in range(2):
                        st(TS(G[:, t, OFF:LP], bank[6 + t][:, 0:T], par[:, layer, PCOL["bg"] + t:PCOL["bg"] + t + 1],
                              0.0, ALU.add, ALU.min))
                    st.wait()
                    TT(G[:, :, OFF:LP], G[:, :, OFF:LP], X[:, :, OFF:LP], ALU.subtract).then_inc(la_dve, 1)
                elif name == "scan":
                    if u == 0:
                        dve.wait_ge(la_dve, N(unit, "gz", 0, "dve"))
                        st(E.memset(S[:], 0.0))
                    else:
                        dve.wait_ge(la_act, N(unit, "pre", 0, "act"))
                    for t in range(2):
                        st(E.tensor_tensor_scan(B[:, t, :], C[:, cc["reset"]], G[:, t, :], 0.0, ALU.mult, ALU.add))
                    st.wait()
                    ref = chunks(B)[:, :, CH // 2 - 1:CH // 2].broadcast_to([P, 2 * NCH, CH])
                    TT(chunks(X), chunks(B), ref, ALU.subtract).then_inc(la_dve, 1)
                elif name == "mul1":
                    dve.wait_ge(la_act, N(unit, "scan", 0, "act"))
                    st(TT(QE[:], QE[:], Q[:], ALU.mult))
                    st(TT(KE[:], KE[:], K[:], ALU.mult))
                    dve.wait_ge(la_act, N(unit, "mul1", 0, "act"))
                    st.wait()
                    TT(Q[:], Q[:], X[:], ALU.mult).then_inc(la_dve, 1)
                elif name == "mul2":
                    dve.wait_ge(la_dve, N(unit, "mul1", 0, "dve"))
                    end = chunks(B)[:, :, CH - 1:CH].broadcast_to([P, 2 * NCH, CH])
                    TT(chunks(X), end, chunks(B), ALU.subtract).then_inc(la_dve, 1)
                elif name == "mul3":
                    dve.wait_ge(la_act, N(unit, "mul2", 0, "act"))
                    TT(K[:], K[:], X[:], ALU.mult).then_inc(la_dve, 1)
                elif name == "kt":
                    dve.wait_ge(la_psum, N(unit, name, i, "pe"))
                    if i == 0:
                        st(CP(KLT[0:META, 0, :], L[0:META, 0:256]))
                        CP(KLT[:, 1, :], L[0:CH, 256:512]).then_inc(la_dve, 1)
                    else:
                        CP(KLT[:, 2:4, :].rearrange("p c d -> p (c d)"), L[0:CH, :]).then_inc(la_dve, 1)
                elif name == "ds":
                    dve.wait_ge(la_psum, N(unit, name, i, "pe"))
                    where = [(2 * i, 0, 64), (2 * i + 1, 64, 128)] if u == 0 else [(i, 0, 128)]
                    for c in range(4):
                        for n, (h, a, b) in enumerate(where):
                            ps = L[a:b, c * P:(c + 1) * P]
                            if c == 0:
                                st(CP(S[a:b, 0, h, :], ps))
                            else:
                                ins = STT(S[a:b, c, h, :], S[a:b, c - 1, h, :], dec[a:b, i, c:c + 1], ps,
                                          ALU.mult, ALU.add)
                                if c == 3 and n == len(where) - 1:
                                    ins.then_inc(la_dve, 1)
                                else:
                                    st(ins)
                        if c < 3:
                            st.wait()
                elif name == "a":
                    dve.wait_ge(la_psum, N(unit, name, i, "pe"))
                    m = C[0:CH, cc["cos"]].bitcast(I32)
                    st(E.copy_predicated(AT[:, i % 2, 0:256], m[:, 0:256], L[0:CH, 0:256]))
                    E.copy_predicated(AT[0:META, i % 2, 256:272], m[0:META, 256:272],
                                      L[0:META, 256:272]).then_inc(la_dve, 1)
                elif name == "n":
                    dve.wait_ge(la_act, N(unit, name, i, "act"))
                    g = par[:, layer, PCOL["glao" if u == 0 else "hgrno"]:][:, 0:1]
                    where = O[:, 0, i, :] if u == 0 else O[:, 1, 2 * (u - 1) + i, :]
                    STT(where, ob[:, i % 2, :], g, rl[:, i % 2, :], ALU.mult, ALU.mult).then_inc(la_dve, 1)

            E.memset(eps[:], EPS).then_inc(zeroed, 1)
            zero_pads()
            dve.wait_ge(par_landed, 16)
            l0, l1 = (par[:, l, PCOL["lb"]:PCOL["lb"] + 4] for l in range(2))
            st(TT(lbt[:, 0, :], l0, l1, ALU.max))
            st.wait()
            st(TT(lbt[:, 1, :], l0, lbt[:, 0, :], ALU.subtract))
            TT(lbt[:, 2, :], l1, lbt[:, 0, :], ALU.subtract).then_inc(lb_sub, 1)
            dve.wait_ge(lb_exp, 1)
            st(TT(lbt[:, 3, :], lbt[:, 1, :], lbt[:, 2, :], ALU.add))
            st.wait()
            st(E.reciprocal(lbt[:, 3, :], lbt[:, 3, :]))
            st.wait()
            for l in range(2):
                st(TT(lbt[:, 1 + l, :], lbt[:, 1 + l, :], lbt[:, 3, :], ALU.mult))
            st.wait()
            st(TT(lbt[:, 3, :], lbt[:, 1, :], lbt[:, 2, :], ALU.add))
            st(TT(lbp[:, 0, 0, :], lbt[:, 1, :], lbt[:, 1, :], ALU.subtract))
            st.wait()
            st(TT(lbp[:, 1, 0, :], lbt[:, 3, :], lbt[:, 1, :], ALU.subtract))
            st.wait()
            TS(lbp[:, :, 1, :], lbp[:, :, 0, :], -1.0, 1.0, ALU.mult, ALU.add).then_inc(lb_ready, 1)
            for k in range(KD):
                dve.wait_ge(x_turned, k + 1)
                CP(hT[:, k, :], bank[2 + k % 2][:, 0:T]).then_inc(h_loaded, 1)
            for g in range(2):
                split_lo(g)
            gains = [par[:, l, PCOL[n]:PCOL[n] + 8] for l in range(2) for n in ("attn", "ffn")]
            norm(0, gains[0], True)
            phase = 1
            for g in range(NG):
                if g + 2 < NG:
                    split_lo(g + 2)
                if g in norm_before:
                    norm(phase, gains[phase], True)
                    if jobs[g][1] == "dq":
                        zero_pads()
                    phase += 1
                for half in range(2):
                    if half == 1:
                        evacuate(g)
                    for s in side.get(2 * g + half, ()):
                        if s[1] in DVE_PART:
                            (mla if s[1] in MLA_NAMES else la)(*s)

            norm(phase, gains[phase], False)
            E.memset(selT[:], 0.0).then_inc(zeroed, 1)
            for b in range(2):
                for half in range(2):
                    dve.wait_ge(turned_h, 2 * b + half + 1)
                    CP(acc[:, b, half * 512:(half + 1) * 512], bank[2 + half][:]).then_inc(acc_loaded, 1)
            dve.wait_ge(logits_ready, 1)
            dve.wait_ge(moe_const, 48)
            R = lambda n: rt[:, n, :, :]
            lg, e1, s1, lg2, e2, s2, cs, gs, tmp = (R(n) for n in range(9))
            for b in range(2):
                st(TT(lg[:, b, :], brb[:], bank[4][:, 8 * b:8 * b + 8], ALU.add))
            st.wait()

            def pick_first(which, values, eq, sel):
                st(E.tensor_reduce(top[:, :, which:which + 1], values, AX.X, ALU.max))
                st.wait()
                st(TT(eq, values, top[:, :, which:which + 1].broadcast_to([P, 2, NE]), ALU.is_equal))
                st.wait()
                for b in range(2):
                    st(E.tensor_tensor_scan(tmp[:, b, :], eq[:, b, :], eq[:, b, :], 0.0, ALU.add, ALU.bypass))
                st.wait()
                st(STT(sel, tmp, 1.0, eq, ALU.is_equal, ALU.mult))
                st.wait()

            pick_first(0, lg, e1, s1)
            st(STT(lg2, s1, -3e38, lg, ALU.mult, ALU.add))
            st.wait()
            pick_first(1, lg2, e2, s2)
            TT(top[:, :, 2], top[:, :, 1], top[:, :, 0], ALU.subtract).then_inc(router_diff, 1)
            TT(cs, s1, s2, ALU.add).then_inc(chosen, 1)
            dve.wait_ge(router_exp, 1)
            st(TS(top[:, :, 3], top[:, :, 2], 1.0, None, ALU.add))
            st.wait()
            st(E.reciprocal(w12[:, :, 0], top[:, :, 3]))
            st.wait()
            st(TT(w12[:, :, 1], w12[:, :, 0], top[:, :, 2], ALU.mult))
            dve.wait_ge(ranked, 1)
            cnt, nb, end, start = (R(9 + n)[:, 0, :] for n in range(4))
            st(CP(cnt, bank[5][:, 16:24]))
            st(CP(R(13), bank[5][:, 0:16].rearrange("p (b e) -> p b e", b=2)))
            st.wait()
            st(TS(nb, cnt, float(P), None, ALU.is_gt))
            st.wait()
            st(STT(nb, cnt, 0.0, nb, ALU.is_gt, ALU.add))
            st.wait()
            st(E.tensor_tensor_scan(end, nb, nb, 0.0, ALU.add, ALU.bypass))
            st.wait()
            st(TT(start, end, nb, ALU.subtract))
            st.wait()
            for b in range(2):
                st(STT(gs[:, b, :], start, float(P), R(13)[:, b, :], ALU.mult, ALU.add))
            st.wait()
            for n, s in ((0, s1), (1, s2)):
                st(TT(tmp, s, gs, ALU.mult))
                st.wait()
                st(E.tensor_reduce(slot[:, :, n:n + 1], tmp, AX.X, ALU.add))
                st.wait()
            item_f = iit[:, 0, :]
            st(E.memset(item_f, 0.0))
            for e in range(NE):
                st.wait()
                st(STT(item_f, MC[0:1, 0:16], end[0:1, e:e + 1], item_f, ALU.is_ge, ALU.add))
            st.wait()
            TS(it_i[:], item_f, float(NE - 1), None, ALU.min).then_inc(items_ready, 1)
            CP(nit_i[:], end[0:1, NE - 1:NE]).then_inc(items_ready, 1)

            def select():
                for b in range(2):
                    st(TS(oh[:, b, :], iota, slot[:, b, 0:1], None, ALU.is_equal))
                    st(TS(selw[:, b, :], iota, slot[:, b, 0:1], w12[:, b, 0:1], ALU.is_equal, ALU.mult))
                    st(TS(ow[:, b, :], iota, slot[:, b, 1:2], w12[:, b, 1:2], ALU.is_equal, ALU.mult))
                st.wait()
                for b in range(2):
                    st(STT(sel[:, b, :], iota, slot[:, b, 1:2], oh[:, b, :], ALU.is_equal, ALU.add))
                TT(selw[:], selw[:], ow[:], ALU.add).then_inc(sel_ready, 1)

            def expert_lo(k, made):
                dve.wait_ge(mhi_made, made)
                TT(mlo[k % MSPLIT][:], mraw[k % MRAW][:], mhi[k % MSPLIT][:].bitcast(F32),
                   ALU.subtract).then_inc(mlo_made, 1)

            def gathered_lo(first):
                for half in range(2):
                    dve.wait_ge(xh_made, first + half)
                    TT(xl[:, 4 * half:4 * half + 4, :].rearrange("p k s -> p (k s)"), bank[4 + half][:],
                       xh[:, 4 * half:4 * half + 4, :].rearrange("p k s -> p (k s)").bitcast(F32),
                       ALU.subtract).then_inc(xl_made, 1)

            select()
            dve.sem_inc(h_made, 2)
            dve.sem_inc(hl_made, 2)
            dve.sem_inc(mlo_made, MRAW)
            n_items = dve.value_load(nit_i[0:1, 0:1], min_val=1, max_val=12)
            for k in range(MSPLIT):
                expert_lo(k, k + 1)
            gathered_lo(1)
            with dve.Fori(0, n_items) as i:
                m = 0

                def own(ins):
                    nonlocal m
                    ins.then_inc(item_step, 1)
                    m += 1

                def own_wait():
                    dve.wait_ge(item_step, i * OWN + m)

                for k in range(ITEM):
                    dve.wait_ge(chunk_done, i * ITEM + (k + 1))
                    if k % 2 == 1 and k < 2 * N_GU:
                        j = k // 2
                        dve.wait_ge(sg_made, i * N_GU + (j + 1))
                        dve.wait_ge(hl_made, i * N_GU + (j + 1))
                        TT(hs[:, j % 2, :], sg[:, j % 2, :], bank[j % 2][:, EC:2 * EC], ALU.mult).then_inc(h_made, 1)
                    expert_lo((k + MSPLIT) % ITEM, i * ITEM + (k + MSPLIT + 1))
                    if k % 2 == 0 and 4 <= k <= 2 * N_GU + 2:
                        j = (k - 4) // 2
                        dve.wait_ge(hh_made, i * N_GU + (j + 1))
                        TT(hl[:, 2 * j:2 * j + 2, :].rearrange("p f s -> p (f s)"), bank[6 + j % 2][:, 0:2 * P],
                           hh[:, 2 * j:2 * j + 2, :].rearrange("p f s -> p (f s)").bitcast(F32),
                           ALU.subtract).then_inc(hl_made, 1)
                    if k in (COMBINE_AT + 1, COMBINE_AT + 3):
                        for q in range(k - COMBINE_AT - 1, k - COMBINE_AT + 1):
                            dve.wait_ge(combined, i * 4 + (q + 1))
                            a = acc[:, q // 2, (q % 2) * 512:(q % 2 + 1) * 512]
                            TT(a, a, bank[4 + q % 2][:], ALU.add).then_inc(acc_added, 1)
                    if k == TURN_AT + 1:
                        dve.wait_ge(sel_turned, i + 1)
                        CP(selT[:].rearrange("p b t -> p (b t)"), bank[4][:, 0:2 * P]).then_inc(selT_ready, 1)
                    if k == TURN_AT + 2:
                        own(TS(slot[:, :, 0:2], slot[:, :, 0:2], float(P), None, ALU.subtract))
                        own_wait()
                        for b in range(2):
                            own(TS(oh[:, b, :], iota, slot[:, b, 0:1], None, ALU.is_equal))
                            own(TS(selw[:, b, :], iota, slot[:, b, 0:1], w12[:, b, 0:1], ALU.is_equal, ALU.mult))
                            own(TS(ow[:, b, :], iota, slot[:, b, 1:2], w12[:, b, 1:2], ALU.is_equal, ALU.mult))
                        own_wait()
                        for b in range(2):
                            own(STT(sel[:, b, :], iota, slot[:, b, 1:2], oh[:, b, :], ALU.is_equal, ALU.add))
                        TT(selw[:], selw[:], ow[:], ALU.add).then_inc(sel_ready, 1)
                    if k == GATHER_AT + 1:
                        gathered_lo(i * 2 + 3)
                assert m == OWN
            for q in range(4):
                dve.wait_ge(combined, n_items * 4 + (q + 1))
                a = acc[:, q // 2, (q % 2) * 512:(q % 2 + 1) * 512]
                TT(a, a, bank[4 + q % 2][:], ALU.add).then_inc(acc_added, 1)

        @block.tensor
        def _(pe):
            MM, TR = pe.matmul, pe.transpose

            def norm(phase):
                pe.wait_ge(norm_sq, phase + 1)
                for k in range(KD):
                    ins = MM(bank[2][:, 0:T], ones, gt[:, k, :], start=k == 0, stop=k == KD - 1)
                ins.then_inc(norm_sum, 1)

            def product(ps, g, k, row, xh_, xl_, first, last, c0=0):
                h, l = hi[g % SPLIT][:, c0:c0 + P], lo[g % SPLIT][:, c0:c0 + P]
                MM(ps, h, xh_, start=first, stop=False)
                MM(ps, h, xl_, start=False, stop=False)
                return MM(ps, l, xh_, start=False, stop=last)

            def stream(g, half):
                layer, kind, i = jobs[g]
                j = of_job[g]
                o = j["out"]
                if half == 0:
                    pe.wait_ge(hi_made, g + 1)
                    pe.wait_ge(lo_made, g + 1)
                if kind == "wo":
                    oo = o + half
                    if oo >= 2:
                        drained(pe, oo - 2)
                    if i % 4 == 0 and half == 0:
                        if i == 0:
                            pe.wait_ge(mla_dve, N(layer, "ot", 3, "dve"))
                        else:
                            pe.wait_ge(silu_done, J(layer, "r" if i == 4 else "hg", 3)["silu"] + 1)
                    for k in range(4):
                        ins = product(bank[oo % 2][:, 0:T], g, k, k, OH[:, k, :], OL[:, k, :], k == 0, k == 3,
                                      k * 256 + half * P)
                    ins.then_inc(stream_done, 1)
                    return
                n = tile_source(layer, kind, i)[1][0]
                first = kind != "fd" or i % 3 == 0
                last = kind != "fd" or i % 3 == 2
                if half == 0 and first and o >= 2:
                    drained(pe, o - 2)
                if kind == "fd" and i == 0 and half == 0:
                    pe.wait_ge(silu_done, J(layer, "fu", NF - 1)["silu"] + 1)
                for k in range(*((0, 4) if half == 0 else (4, n))):
                    if kind == "fd":
                        f = 8 * (i % 3) + k
                        xx = HH[:, f, :], HL[:, f, :]
                    else:
                        if g in need_u:
                            pe.wait_ge(u_ready, 8 * need_u[g] + k + 1)
                        xx = UH[:, k, :], UL[:, k, :]
                    ins = product(bank[o % 2][:, 0:T], g, k, k, *xx, first and k == 0, last and k == n - 1, k * P)
                if half == 1:
                    ins.then_inc(stream_done, 1)

            def mla(layer, name, i):
                p = i % 2
                Ma, Mb = bank[2 + 2 * p], bank[3 + 2 * p]
                if name == "ss":
                    drained(pe, J(layer, "dkv", 0)["out"])
                    drained(pe, J(layer, "dkv", 0)["out"] - 1)
                    MM(bank[2][:, 0:T], ones, gt[:, 0, :], start=True, stop=False)
                    MM(bank[2][:, 0:T], ones, gt[:, 1, :], start=False, stop=True)
                    MM(bank[3][:, 0:T], ones, gt[:, 2, :], start=True, stop=True).then_inc(mla_psum, 1)
                elif name == "vm":
                    pe.wait_ge(mla_dve, N(layer, "ss", 0, "dve"))
                    pe.wait_ge(small_landed, 48 * (layer + 1))
                    vw = wukv[:].rearrange("p (h c) -> p h c", h=HEADS)[:, :, NOPE:]
                    for b, (c0, n) in enumerate(BLOCKS):
                        ins = MM(bank[(4, 5, 2)[b]][0:n, :].rearrange("p (h c) -> p h c", h=HEADS),
                                 dqT[:, 2, c0:c0 + n], vw, start=True, stop=True)
                    ins.then_inc(mla_psum, 1)
                elif name == "qk":
                    if i < 2:
                        pe.wait_ge(mla_act, N(layer, "vm", 0, "act"))
                    else:
                        pe.wait_ge(mla_dve, N(layer, "pv", i - 2, "dve"))
                    for t in range(2):
                        MM(Ma[0:QK, 0:T], wuq[:, t, i * QK:(i + 1) * QK], dqT[:, t, :], start=t == 0, stop=t == 1)
                    MM(Mb[0:NOPE, 0:T], wukv[:, i * P:i * P + NOPE], dqT[:, 2, :],
                       start=True, stop=True).then_inc(mla_psum, 1)
                elif name == "nrm":
                    pe.wait_ge(mla_act, N(layer, "qk", i, "act"))
                    pe.wait_ge(mla_dve, N(layer, "qk", i, "dve"))
                    MM(Ma[0:QK, 0:T], ones[0:QK, 0:QK], qsq[:, p, 0, :], start=True, stop=True)
                    MM(Mb[0:QK, 0:T], ones[0:QK, 0:QK], qsq[:, p, 1, :], start=True, stop=True).then_inc(mla_psum, 1)
                elif name == "rot":
                    pe.wait_ge(mla_dve, N(layer, "nrm", i, "dve"))
                    R_ = C[NOPE:QK, cc["rot"]]
                    MM(Ma[NOPE:QK, 0:T], R_, qk[NOPE:QK, p, 0, :], start=True, stop=True)
                    MM(Mb[NOPE:QK, 0:T], R_, qk[NOPE:QK, p, 1, :], start=True, stop=True).then_inc(mla_psum, 1)
                elif name == "sc":
                    pe.wait_ge(mla_dve, N(layer, "rot", i, "dve"))
                    q_, k_ = qk[:, p, 0, :], qk[:, p, 1, :]
                    MM(Ma[:, 0:272], q_[:, 144:272], k_, start=True, stop=True)
                    MM(Ma[:, 272:416], q_[:, 16:144], k_[:, 0:144], start=True, stop=True)
                    MM(Ma[0:META, 416:432], q_[:, 0:16], k_[:, 0:16], start=True, stop=True).then_inc(mla_psum, 1)
                elif name == "pt":
                    pe.wait_ge(mla_act, N(layer, "sc", i, "act"))
                    TR(Mb[:, 0:128], pr[:, p, 16:144], ident)
                    TR(Mb[:, 128:256], pr[:, p, 144:272], ident)
                    TR(Mb[:, 256:384], pr[:, p, 288:416], ident)
                    TR(Ma[0:META, 0:128], pr[:, p, 0:16], ident)
                    TR(Ma[0:META, 128:256], pr[:, p, 272:288], ident)
                    TR(Ma[0:META, 256:272], pr[0:META, p, 416:432], ident[0:META, 0:META]).then_inc(mla_psum, 1)
                elif name == "pv":
                    pe.wait_ge(mla_act, N(layer, "pt", i, "act"))
                    pe.wait_ge(mla_dve, N(layer, "pt", i, "dve"))
                    c = slice(i * VDIM, (i + 1) * VDIM)
                    MM(Ma[:, 0:VDIM], ptm[:, p, 0:128], vtok[0:META, 0, c], start=True, stop=False)
                    MM(Ma[:, 0:VDIM], ptf[:, p, 0:128], vtok[:, 1, c], start=False, stop=False)
                    MM(Ma[:, 0:VDIM], ptf[:, p, 128:256], vtok[:, 2, c], start=False, stop=True)
                    MM(Mb[:, 0:VDIM], ptm[:, p, 128:256], vtok[0:META, 0, c], start=True, stop=False)
                    MM(Mb[:, 0:VDIM], ptf[:, p, 256:384], vtok[:, 1, c], start=False, stop=True)
                    MM(Mb[0:META, VDIM:2 * VDIM], ptm[:, p, 256:272], vtok[0:META, 0, c],
                       start=True, stop=True).then_inc(mla_psum, 1)
                elif name == "ot":
                    pe.wait_ge(mla_dve, N(layer, "pv", HEADS - 1, "dve"))
                    M, c = bank[2 + i], slice(i * P, (i + 1) * P)
                    TR(M[:, 16:144], otok[:, 1, c], ident)
                    TR(M[:, 144:272], otok[:, 2, c], ident)
                    TR(M[:, 0:16], otok[0:META, 0, c], ident[0:META, 0:META]).then_inc(mla_psum, 1)

            def la(unit, name, i):
                layer, u = divmod(unit, 3)
                L = bank[6 + i % 2]
                nh = heads_of(unit)
                if name == "gz":
                    drained(pe, J(layer, "gd", 0)["out"])
                    pe.wait_ge(small_landed, 48 * (layer + 1))
                    if layer:
                        pe.wait_ge(la_dve, N(unit - 1, "n", 1, "dve"))
                    for t in range(2):
                        ins = MM(bank[6 + t][:, 0:T], wg2[:, t * P:(t + 1) * P], gdT[:], start=True, stop=True)
                    ins.then_inc(la_psum, 1)
                elif name == "vt":
                    if i == 0:
                        o = J(layer, "v", 3 if u == 0 else 5 + 2 * (u - 1))["out"]
                        drained(pe, o)
                        drained(pe, o - 1)
                    if u == 0 and i < 2:
                        pe.wait_ge(la_dve, N(unit, "gz", 0, "dve"))
                    elif i >= 2:
                        pe.wait_ge(la_act, N(unit, "vt", i - 2, "act"))
                    else:
                        pe.wait_ge(la_act, N(unit - 1, "n", heads_of(unit - 1) - 2 + i, "act"))
                    _, c = chunk_cols(i)
                    rows = c.stop - c.start
                    for h in range(nh):
                        ins = TR(L[0:rows, h * P:(h + 1) * P], VT[:, h, c], ident)
                    ins.then_inc(la_psum, 1)
                elif name == "kt":
                    pe.wait_ge(la_act, N(unit, "vt", 4 if i == 0 else 3, "act"))
                    pe.wait_ge(la_dve, N(unit, "mul3", 0, "dve"))
                    for c in (2 * i, 2 * i + 1):
                        cols, _ = chunk_cols(c)
                        rows = cols.stop - cols.start
                        for t in range(2):
                            ins = TR(L[0:rows, (c % 2) * 256 + t * P:(c % 2) * 256 + (t + 1) * P], K[:, t, cols], ident)
                    ins.then_inc(la_psum, 1)
                elif name == "ds":
                    pe.wait_ge(la_dve, N(unit, "kt", 1, "dve"))
                    pe.wait_ge(la_act, N(unit, "vt", 4, "act"))
                    where = [(2 * i, 0, 64), (2 * i + 1, 64, 128)] if u == 0 else [(i, 0, 128)]
                    for c in range(4):
                        rows = META if c == 0 else CH
                        for h, a, b in where:
                            ins = MM(L[a:b, c * P:(c + 1) * P], KLT[0:rows, c, i * P + a:i * P + b],
                                     V[0:rows, c, h * P:(h + 1) * P], start=True, stop=True)
                    ins.then_inc(la_psum, 1)
                elif name == "a":
                    if i < 2:
                        pe.wait_ge(la_dve, N(unit, "ds", 1, "dve"))
                    else:
                        pe.wait_ge(la_act, N(unit, "n", i - 2, "act"))
                    t, a, b = (i // 2, 64 * (i % 2), 64 * (i % 2) + 64) if u == 0 else (i, 0, P)
                    for c in range(1, NCH):
                        MM(L[0:CH, (c - 1) * CH:c * CH], KE[a:b, t, c * CH:(c + 1) * CH],
                           QE[a:b, t, c * CH:(c + 1) * CH], start=True, stop=True)
                    MM(L[0:META, 256:272], KE[a:b, t, OFF:CH], QE[a:b, t, OFF:CH],
                       start=True, stop=True).then_inc(la_psum, 1)
                elif name == "o":
                    pe.wait_ge(la_dve, N(unit, "a", i, "dve"))
                    t = i // 2 if u == 0 else i
                    v = lambda c, rows: V[0:rows, c, i * P:(i + 1) * P]
                    MM(L[:, 0:META], v(0, META), AT[0:META, i % 2, 256:272], start=True, stop=True)
                    for c in range(1, NCH):
                        ps = L[:, META + (c - 1) * CH:META + c * CH]
                        MM(ps, v(c, CH), AT[:, i % 2, (c - 1) * CH:c * CH], start=True, stop=False)
                        ins = MM(ps, S[:, c - 1, i, :], Q[:, t, c * CH:(c + 1) * CH], start=False, stop=True)
                    ins.then_inc(la_psum, 1)
                elif name == "n":
                    pe.wait_ge(la_act, N(unit, "o", i, "act"))
                    MM(L[:, 0:T], ones, osq[:, i % 2, :], start=True, stop=True).then_inc(la_psum, 1)

            pe.wait_ge(x_landed, 32)
            pe.wait_ge(const_landed, 16)
            pe.wait_ge(zeroed, 1)
            gx = gt[:].rearrange("p k t -> p (k t)")
            mxx = mixed[:].rearrange("p k t -> p (k t)")
            for k in range(KD):
                if k >= 2:
                    pe.wait_ge(h_loaded, k - 1)
                b_ = bank[2 + k % 2]
                TR(b_[:, 16:144], gx[:, k * P:(k + 1) * P], ident)
                TR(b_[:, 144:272], gx[:, D + k * P:D + (k + 1) * P], ident)
                TR(b_[:, 0:16], mxx[0:META, k * P:(k + 1) * P], ident[0:META, 0:META]).then_inc(x_turned, 1)
            norm(0)
            phase = 1
            for g in range(NG):
                if g in norm_before:
                    norm(phase)
                    phase += 1
                for half in range(2):
                    stream(g, half)
                    for s in side.get(2 * g + half, ()):
                        if s[1] in PE_PART:
                            (mla if s[1] in MLA_NAMES else la)(*s)

            norm(phase)
            pe.wait_ge(u_whole, 1)
            pe.wait_ge(moe_const, 48)
            pe.wait_ge(zeroed, 2)
            for b in range(2):
                for k in range(KD):
                    ins = MM(bank[4][:, 8 * b:8 * b + 8], mixed[:, k, META + b * P:META + (b + 1) * P], wr[:, k, :],
                             start=k == 0, stop=k == KD - 1)
            ins.then_inc(logits_ready, 1)
            for b in range(2):
                for half in range(2):
                    if b:
                        pe.wait_ge(utok_made, half + 1)
                        pe.wait_ge(acc_loaded, half + 1)
                    for src, bk, done in ((mixed, bank[half], turned_u), (hT, bank[2 + half], turned_h)):
                        for k in range(4):
                            ins = TR(bk[:, k * P:(k + 1) * P], src[:, 4 * half + k, META + b * P:META + (b + 1) * P], ident)
                        ins.then_inc(done, 1)
            pe.wait_ge(chosen, 1)
            cs = rt[:, 6, :, :]
            MM(bank[5][:, 0:8], tri, cs[:, 0, :], start=True, stop=True)
            for c0, last_w in ((8, tri), (16, ones)):
                MM(bank[5][:, c0:c0 + 8], ones, cs[:, 0, :], start=True, stop=False)
                ins = MM(bank[5][:, c0:c0 + 8], last_w, cs[:, 1, :], start=False, stop=True)
            ins.then_inc(ranked, 1)
            pe.wait_ge(items_ready, 2)
            n_items = pe.value_load(nit_i[0:1, 0:1], min_val=1, max_val=12)

            def gather():
                for half in range(2):
                    for k in range(4):
                        for b in range(2):
                            c0 = (4 * half + k) * P
                            ins = MM(bank[4 + half][:, k * P:(k + 1) * P], utok[:, b, c0:c0 + P], sel[:, b, :],
                                     start=b == 0, stop=b == 1)
                    ins.then_inc(x_gathered, 1)

            def combine(q):
                return MM(bank[4 + q % 2][:], selT[:, q // 2, :], ys[:, (q % 2) * 512:(q % 2 + 1) * 512],
                          start=True, stop=True).then_inc(combined, 1)

            pe.wait_ge(utok_made, 4)
            pe.wait_ge(acc_loaded, 4)
            pe.wait_ge(sel_ready, 1)
            gather()
            with pe.Fori(0, n_items) as i:
                for k in range(ITEM):
                    pe.wait_ge(mhi_made, i * ITEM + (k + 1))
                    pe.wait_ge(mlo_made, i * ITEM + (MRAW + k + 1))
                    h, l = mhi[k % MSPLIT], mlo[k % MSPLIT]
                    if k < 2 * N_GU:
                        j = k // 2
                        if k == 0:
                            pe.wait_ge(xl_made, i * 2 + 2)
                        if k % 2 == 0:
                            pe.wait_ge(h_made, i * N_GU + (j + 1))
                        ps = bank[j % 2][:, (k % 2) * EC:(k % 2 + 1) * EC]
                        for r in range(KD):
                            c = slice(r * EC, (r + 1) * EC)
                            MM(ps, xh[:, r, :], h[:, c], start=r == 0, stop=False)
                            MM(ps, xh[:, r, :], l[:, c], start=False, stop=False)
                            ins = MM(ps, xl[:, r, :], h[:, c], start=False, stop=r == KD - 1)
                    else:
                        d = k - 2 * N_GU
                        pe.wait_ge(hl_made, i * N_GU + (d + 3))
                        if d == 0:
                            pe.wait_ge(y_out, i * 2 + 2)
                        for f in range(2):
                            for n in range(2):
                                c = slice(f * D + n * 512, f * D + (n + 1) * 512)
                                ps = bank[2 + n][:]
                                MM(ps, hh[:, 2 * d + f, :], h[:, c], start=d == 0 and f == 0, stop=False)
                                MM(ps, hh[:, 2 * d + f, :], l[:, c], start=False, stop=False)
                                ins = MM(ps, hl[:, 2 * d + f, :], h[:, c], start=False, stop=d == N_DN - 1 and f == 1)
                    ins.then_inc(chunk_done, 1)
                    if k % 2 == 1 and 3 <= k <= 2 * N_GU + 1:
                        j = (k - 3) // 2
                        pe.wait_ge(h_made, i * N_GU + (j + 3))
                        pe.wait_ge(hl_made, i * N_GU + (j + 1))
                        for f in range(2):
                            ins = TR(bank[6 + j % 2][:, f * P:(f + 1) * P], hs[:, j % 2, f * P:(f + 1) * P], ident)
                        ins.then_inc(h_turned, 1)
                    if k == COMBINE_AT:
                        pe.wait_ge(y_out, i * 2 + 2)
                        for q in range(2):
                            combine(q)
                    if k == COMBINE_AT + 2:
                        for q in range(2, 4):
                            pe.wait_ge(acc_added, i * 4 + (q - 1))
                            combine(q)
                    if k == TURN_AT:
                        pe.wait_ge(acc_added, i * 4 + 4)
                        pe.wait_ge(sel_ready, i + 1)
                        for b in range(2):
                            ins = TR(bank[4][:, b * P:(b + 1) * P], selw[:, b, :], ident)
                        ins.then_inc(sel_turned, 1)
                    if k == GATHER_AT:
                        pe.wait_ge(sel_ready, i + 2)
                        pe.wait_ge(selT_ready, i + 1)
                        gather()
            pe.wait_ge(y_out, n_items * 2 + 2)
            pe.wait_ge(xl_made, n_items * 2 + 2)
            for q in range(4):
                if q >= 2:
                    pe.wait_ge(acc_added, n_items * 4 + (q - 1))
                combine(q)


CONSTS = [("ident", P), ("ones", P), ("rot", ROPE), ("cos", T), ("sin", T), ("smask", 432),
          ("reset", LP)]


def constants():
    c = {n: np.zeros((P, w), np.float32) for n, w in CONSTS}
    p = np.arange(P)
    c["ident"][p, p] = 1
    c["ones"][:] = 1
    half = ROPE // 2
    for j in range(half):
        c["rot"][NOPE + half + j, j] = -1
        c["rot"][NOPE + j, half + j] = 1
    inv = np.float32(10000.0) ** (-np.arange(half, dtype=np.float32) / np.float32(half))
    ang = np.arange(T, dtype=np.float32)[None, :] * inv[:, None].astype(np.float32)
    c["cos"][NOPE:QK] = np.concatenate([np.cos(ang)] * 2)
    c["sin"][NOPE:QK] = np.concatenate([np.sin(ang)] * 2)
    for c0, q0, n in ((0, META + P, T), (T, META, META + P), (T + META + P, 0, META)):
        c["smask"][:, c0:c0 + n] = np.where(np.arange(n)[None, :] <= q0 + p[:, None], 0, NEG)
    j, i = np.arange(CH)[:, None], np.arange(CH)[None, :]
    c["cos"][0:CH, 0:256] = np.tile(j <= i, (1, 4))
    c["cos"][0:META, 256:272] = (j <= i)[0:META, 0:META]
    c["reset"][:] = (np.arange(LP) % CH != 0)[None, :]
    out = np.concatenate([c[n] for n, _ in CONSTS], 1).astype(np.float32)
    moe = np.concatenate([np.tile(np.arange(P)[None, :], (P, 1)), p[:, None] < p[None, :],
                          np.zeros((P, P))], 1).astype(np.float32)
    return out, moe


WEIGHTS = ["w_in", "w_mla_uq", "w_mla_ukv", "w_gla_g2", "w_mla_o", "w_gla_o", "w_hgrn_o", "w_out", "w_ff_gate",
           "w_ff_up", "w_ff_down", "w_router", "b_router", "w_exp_gate", "w_exp_up", "w_exp_down"]


def lay_out(a):
    ins = {n: np.ascontiguousarray(a[n]) for n in WEIGHTS + ["x", "meta_tokens"]}
    par = np.zeros((P, DEPTH, NPAR), np.float32)
    src = dict(attn="attn_norm", ffn="ffn_norm", cq="mla_cq_norm", ckv="mla_ckv_norm", qn="mla_q_norm",
               kn="mla_k_norm", bg="b_gla_g", glao="gla_o_norm", hgrno="hgrn_o_norm", lb="hgrn_lower_bounds")
    for name, key in src.items():
        v = np.asarray(a[key])
        for layer in range(DEPTH):
            rows = min(P, v.shape[1])
            cols = v[layer].reshape(-1, rows).T
            par[0:rows, layer, PCOL[name]:PCOL[name] + cols.shape[1]] = cols
    ins["params"] = par
    ins["consts"], ins["moe_consts"] = constants()
    return ins


def kernel(**inputs):
    import concourse.bacc as _bacc
    from concourse.bass_utils import run_bass_kernel_spmd as _run

    nc = _bacc.Bacc("TRN2", target_bir_lowering=False, num_devices=1)
    arrays = {f"in_{n}": a for n, a in lay_out(inputs).items()}
    A = {n[3:]: nc.dram_tensor(n, a.shape, mybir.dt.from_np(a.dtype), kind="ExternalInput").ap()
         for n, a in arrays.items()}
    out = nc.dram_tensor("out", (1, SEQ, D), F32, kind="ExternalOutput").ap()
    bass_hybrid_trunk(nc, A, out)
    return _run(nc, [arrays], core_ids=[0]).results[0]["out"]
```

```python
from contextlib import ExitStack

import concourse.bass as bass
import numpy as np
from concourse import mybir

F32, F32R, I32 = mybir.dt.float32, mybir.dt.float32r, mybir.dt.int32
ALU = mybir.AluOpType
ACT = mybir.ActivationFunctionType
AX = mybir.AxisListType

P = 128
D = 1024
KD = D // P
META = 16
SEQ = 256
T = META + SEQ
DEPTH = 2
EPS = 1e-6
NEG = -1e30
GUARD = 40.0

HEADS, NOPE, ROPE, VDIM = 8, 64, 32, 64
QK = NOPE + ROPE
CH = 64
NCH = 5
LP = NCH * CH
OFF = CH - META
GLA_DK = 64
FF = 2816
NF = FF // P
NE = 8
DE = 3584
COL = dict(dq=0, dkv=256, kr=384 - 64, gq=416, gk=672, gv=928, gd=1440, r=1456,
           hq=1968, hf=2480, hi=2992, hg=3504, gate=4016)
BLOCKS = ((0, META), (META, P), (META + P, P))

RAW, HI, LOOK, LOOK_LO = 6, 4, 3, 2
MRAW, MHI, MLOOK = 7, 6, 4
EC = 256
N_GU = DE // EC
N_DN = DE // P // 2
ITEM = 2 * N_GU + N_DN
COMBINE_AT, TURN_AT, GATHER_AT = 3, 9, 34
OWN = 8

PCOL = {}


def param_columns():
    at = 0
    for name, n in (("attn", 8), ("ffn", 8), ("cq", 2), ("ckv", 1), ("qn", 1), ("kn", 1), ("bg", 2),
                    ("glao", 1), ("hgrno", 1), ("lb", 4)):
        PCOL[name] = at
        at += n
    return at


NPAR = param_columns()


def chunk_cols(c):
    if c == 0:
        return slice(OFF, CH), slice(0, META)
    return slice(c * CH, (c + 1) * CH), slice(META + (c - 1) * CH, META + c * CH)


def live(layer, kind):
    return slice(META if layer == DEPTH - 1 and kind in ("gate", "r", "hg", "wo", "wout") else 0, T)


def layer_jobs(layer):
    def run(kind, *which):
        return [(kind, i) for i in which]

    jobs = run("dq", 0, 1) + run("dkv", 0) + run("kr", 0) + run("gd", 0) + run("gq", 0, 1) + run("gk", 0, 1)
    jobs += run("v", 0, 1, 2, 3)
    jobs += run("gate", *range(8, 16)) + run("gate", *range(16, 20))
    jobs += run("r", 0, 1, 2, 3) + run("f", 0, 1) + run("q", 0, 1) + run("v", 4, 5)
    jobs += run("wo", 4, 5, 6, 7) + run("gate", *range(20, 24))
    jobs += run("f", 2, 3) + run("q", 2, 3) + run("v", 6, 7)
    jobs += run("hg", 0, 1) + run("gate", *range(6))
    jobs += run("hg", 2, 3) + run("gate", 6) + run("wo", 8, 9, 10, 11) + run("gate", 7)
    jobs += run("wo", 0, 1, 2, 3) + run("wout", *range(8))
    return [(layer, k, i) for k, i in jobs]


def ff_jobs(layer):
    jobs = []
    for f in range(NF):
        jobs += [("fg", f), ("fu", f)]
    jobs += [("fd", 3 * m + j) for m in range(8) for j in range(3)]
    return [(layer, k, i) for k, i in jobs]


def mla_steps(layer):
    out = [("ss", 0), ("vm", 0)]
    for h in range(0, HEADS, 2):
        for s in ("qk", "nrm", "rot", "sc", "pt", "pv"):
            out += [(s, h), (s, h + 1)]
    return [(layer, s, i) for s, i in out + [("ot", t) for t in range(4)]]


def la_steps(layer, unit):
    if unit == 0:
        at = [("gz", 0, 3), ("scan", 0, 5), ("mul1", 0, 10), ("mul2", 0, 12), ("mul3", 0, 14)]
        vt = 20
    else:
        at = [("pre", 0, 5), ("scan", 0, 6), ("mul1", 0, 9), ("mul2", 0, 11), ("mul3", 0, 12)]
        vt = 13
    at += [("vt", c, vt + c) for c in range(NCH)]
    late = vt + NCH + (unit == 0)
    at += [("kt", 0, late), ("kt", 1, late + 1), ("ds", 0, late + 2), ("ds", 1, late + 3)]
    head = late + 5
    for h in range(0, 4 if unit == 0 else 2, 2):
        for s in ("a", "o", "n"):
            at += [(s, h, head), (s, h + 1, head + 1)]
            head += 2
    return [((3 * layer + unit, s, i), n) for s, i, n in at]


LATE = dict(ss=(0, 1), vm=(1, 0), qk=(0, 1), nrm=(0, 1), rot=(0, 2), sc=(2, 1), pt=(1, 1), pv=(0, 1),
            gz=(0, 1), scan=(1, 0), mul1=(0, 1), mul2=(1, 0), mul3=(0, 1), vt=(0, 0), kt=(0, 0), n=(0, 0))


def build_schedule():
    jobs = []
    side = {}
    for layer in range(DEPTH):
        g0 = len(jobs)
        lj = layer_jobs(layer)
        kinds = [(k, i) for _, k, i in lj]
        jobs += lj
        mla = mla_steps(layer)
        at = 2 * (g0 + kinds.index(("kr", 0))) + 2
        end = 2 * (g0 + kinds.index(("wo", 11))) + 1
        heads = [s for s in mla if s[1] != "ot"]
        for n, s in enumerate(heads):
            side.setdefault(at + n * (end - at) // len(heads), []).append(s)
        for s in mla[len(heads):]:
            side.setdefault(end + s[2] // 2, []).append(s)
        for unit, first in enumerate((("gd", 0), ("f", 0), ("f", 2))):
            for s, n in la_steps(layer, unit):
                side.setdefault(2 * (g0 + kinds.index(first)) + n, []).append(s)
        if layer % 2 == 0:
            jobs += ff_jobs(layer)
    order = [(slot, s) for slot in sorted(side) for s in side[slot]]
    shares = dict(pe={}, act={}, dve={})
    for slot, s in order:
        for engine, late in zip(shares, (0, *LATE.get(s[1], (0, 0)))):
            shares[engine].setdefault(slot + late, []).append(s)
    return jobs, shares


def bass_hybrid_trunk(nc, A, out):
    jobs, shares = build_schedule()
    NG = len(jobs)

    parts, outputs, of_job = 0, 0, []
    nexp, nsilu, ngate = 0, 0, 0
    for layer, kind, i in jobs:
        n = 2 if kind == "wo" else 1
        j = dict(part=parts, parts=n, out=outputs, exp=nexp, silu=nsilu, gate=ngate)
        parts += n
        outputs += n if kind != "fd" else int(i % 3 == 2)
        nexp += kind in ("q", "r", "hg")
        ngate += kind == "gate"
        nsilu += kind in ("q", "r", "hg", "fu")
        of_job.append(j)
    place = {job: g for g, job in enumerate(jobs)}

    def J(layer, kind, i):
        return of_job[place[(layer, kind, i)]]

    PE_PART = {"ss", "vm", "qk", "nrm", "rot", "sc", "pt", "pv", "ot", "gz", "vt", "kt", "ds", "a", "o", "n"}
    ACT_PART = {"ss", "vm", "qk", "nrm", "sc", "pt", "ot", "gz", "pre", "scan", "mul1", "mul2", "vt", "o", "n"}
    DVE_PART = {"ss", "qk", "nrm", "rot", "sc", "pt", "pv", "ot", "gz", "scan", "mul1", "mul2", "mul3", "kt",
                "ds", "a", "n"}
    number = {}
    count = dict(mla=[0, 0, 0], la=[0, 0, 0])
    MLA_NAMES = {"ss", "vm", "qk", "nrm", "rot", "sc", "pt", "pv", "ot"}
    for e, (engine, have) in enumerate(zip(shares, (PE_PART, ACT_PART, DVE_PART))):
        for slot in sorted(shares[engine]):
            for s in shares[engine][slot]:
                c = count["mla" if s[1] in MLA_NAMES else "la"]
                c[e] += s[1] in have
                number.setdefault(s, [0, 0, 0])[e] = c[e]

    def N(where, name, i, engine):
        return number[(where, name, i)][("pe", "act", "dve").index(engine)]

    ORDER = {1: 0, 2: 1, 0: 2}

    def mixed_by(layer, b, m):
        return 16 * layer + 8 * (ORDER[b] - 1) + m + 1

    def heads_of(unit):
        return 4 if unit % 3 == 0 else 2

    with ExitStack() as ctx:
        def sb(name, shape, dt=F32, c=ctx):
            return c.enter_context(nc.sbuf_tensor(name, shape, dt))

        def sem(name):
            return ctx.enter_context(nc.semaphore(name))

        bank = [ctx.enter_context(nc.psum_tensor(f"bank{i}", [P, 512], F32)) for i in range(8)]

        hT = sb("hT", [P, KD, T])
        mixed = sb("mixed", [P, KD, T])
        rr = sb("rr", [P, T])
        C = sb("C", [P, A["consts"].shape[1]])
        par = sb("par", [P, DEPTH, NPAR])
        lbp = sb("lbp", [P, DEPTH, 2, 4])
        lbt = sb("lbt", [P, 4, 4])
        eps = sb("eps", [P, 1])
        guard = sb("guard", [P, 1])

        def gate_of(b, m):
            return (O[:, m // 4, m % 4, :], mixed[:, m, :], gt[:, m, :])[b]

        cc = {}
        at = 0
        for name, n in CONSTS:
            cc[name] = slice(at, at + n)
            at += n
        ident, ones = C[:, cc["ident"]], C[:, cc["ones"]]

        x_in = mixed[:].rearrange("p k t -> p (k t)")[:, 0:2 * D].rearrange("p (b d) -> p b d", b=2)
        mix = ExitStack()
        gt = sb("gt", [P, KD, T], c=mix)
        landing = ExitStack()
        raw = [sb(f"raw{i}", [P, 1024], c=landing) for i in range(RAW)]
        landing.close()
        lo = [sb(f"lo{i}", [P, 1024], F32R, mix) for i in range(RAW)]
        hi = [sb(f"hi{i}", [P, 1024], F32R, mix) for i in range(HI)]
        UH = sb("UH", [P, KD, T], F32R, mix)
        UL = sb("UL", [P, KD, T], F32R, mix)
        ez = sb("ez", [P, 2, T], c=mix)

        tok = ExitStack()
        OH = sb("OH", [P, 4, T], F32R, tok)
        OL = sb("OL", [P, 4, T], F32R, tok)
        Q, K, G, B, X, QE, KE = (sb(n, [P, 2, LP], c=tok) for n in ("Q", "K", "G", "B", "X", "QE", "KE"))
        dec = sb("dec", [P, 2, NCH], c=tok)
        gdT = sb("gdT", [16, T], c=tok)
        wg2 = sb("wg2", [16, 256], c=tok)
        VT = sb("VT", [P, 4, T], c=tok)
        V = sb("V", [CH, NCH, 512], c=tok)
        KLT = sb("KLT", [CH, 4, 256], c=tok)
        S = sb("S", [P, 4, 4, P], c=tok)
        AT = sb("AT", [CH, 2, T], c=tok)
        ob = sb("ob", [P, 2, T], c=tok)
        osq = sb("osq", [P, 2, T], c=tok)
        rl = sb("rl", [P, 2, T], c=tok)
        O = sb("O", [P, 2, 4, T], c=tok)
        dqT = sb("dqT", [P, 3, T], c=tok)
        rin = gt[:, 3:5, :]
        wuq = sb("wuq", [P, 2, HEADS * QK], c=tok)
        wukv = sb("wukv", [P, HEADS * (NOPE + VDIM)], c=tok)
        vtok = sb("vtok", [P, 3, 512], c=tok)
        qk = sb("qk", [QK, 2, 2, T], c=tok)
        kr_keep = sb("kr_keep", [QK, T], c=tok)
        qsq = sb("qsq", [QK, 2, 2, T], c=tok)
        pr = sb("pr", [P, 2, 432], c=tok)
        mx = sb("mx", [P, 2, 3], c=tok)
        sm = sb("sm", [P, 2, 3], c=tok)
        ptf = sb("ptf", [P, 2, 384], c=tok)
        ptm = sb("ptm", [META, 2, T], c=tok)
        otok = sb("otok", [P, 3, 512], c=tok)
        tok.close()
        dense = ExitStack()
        HH = sb("HH", [P, NF, T], F32R, dense)
        HL = sb("HL", [P, NF, T], F32R, dense)
        dense.close()
        mix.close()

        mhi_last = sb("mhi_last", [P, 2048], F32R)
        hh = sb("hh", [P, DE // P, P], F32R)
        hl = sb("hl", [P, DE // P, P], F32R)
        xh = sb("xh", [P, KD, P], F32R)
        xl = sb("xl", [P, KD, P], F32R)
        utok = sb("utok", [P, 2, D])
        acc = sb("acc", [P, 2, D])
        sg = sb("sg", [P, 2, EC])
        hs = sb("hs", [P, 2, EC])
        ys = sb("ys", [P, D])
        mlanding = ExitStack()
        mraw = [sb(f"mraw{i}", [P, 2048], c=mlanding) for i in range(MRAW)]
        mlanding.close()
        mlo = [sb(f"mlo{i}", [P, 2048], F32R) for i in range(MRAW)]
        mhi = [sb(f"mhi{i}", [P, 2048], F32R) for i in range(MHI - 1)] + [mhi_last]
        sel = sb("sel", [P, 2, P])
        selw = sb("selw", [P, 2, P])
        selT = sb("selT", [P, 2, P])
        MC = sb("MC", [P, P * 3])
        iota, tri = MC[:, 0:P], MC[:, P:2 * P]
        wr = sb("wr", [P, KD, NE])
        brb = sb("brb", [P, NE])
        rt = sb("rt", [P, 14, 2, NE])
        slot, top, w12 = sb("slot", [P, 2, 2]), sb("top", [P, 2, 4]), sb("w12", [P, 2, 2])
        oh, ow = sb("oh", [P, 2, P]), sb("ow", [P, 2, P])
        iit = sb("iit", [1, 16 * NE])
        item_f = sb("item_f", [1, 16])
        it_i = sb("it_i", [1, 16], I32)
        nit_i = sb("nit_i", [1, 2], I32)

        landed = [sem(f"landed{i}") for i in range(RAW)]
        meta_landed, const_landed, par_landed, small_landed = (
            sem("meta_landed"), sem("const_landed"), sem("par_landed"), sem("small_landed"))
        x_landed = [sem(f"x_landed{i}") for i in range(2)]
        small_used = sem("small_used")
        zeroed = sem("zeroed")
        hi_made, lo_made = sem("hi_made"), sem("lo_made")
        stream_done = sem("stream_done")
        bank_free = [sem("bank0_free"), sem("bank1_free")]
        x_turned, h_loaded = sem("x_turned"), sem("h_loaded")
        norm_sq, norm_sum, norm_r, u_ready = sem("norm_sq"), sem("norm_sum"), sem("norm_r"), sem("u_ready")
        logit_read, exp_made, silu_done = sem("logit_read"), sem("exp_made"), sem("silu_done")
        mix_done, mixed_hi = sem("mix_done"), sem("mixed_hi")
        f_sig, gate_made = sem("f_sig"), sem("gate_made")
        f_ready, lb_exp, lb_sub, lb_ready = sem("f_ready"), sem("lb_exp"), sem("lb_sub"), sem("lb_ready")
        mla_psum, mla_act, mla_dve = sem("mla_psum"), sem("mla_act"), sem("mla_dve")
        la_psum, la_act, la_dve = sem("la_psum"), sem("la_act"), sem("la_dve")
        act_step, dve_step = sem("act_step"), sem("dve_step")
        mlanded = [sem(f"mlanded{i}") for i in range(MRAW)]
        moe_const, turned_u, turned_h = sem("moe_const"), sem("turned_u"), sem("turned_h")
        u_whole, u_hi = sem("u_whole"), sem("u_hi")
        utok_made, acc_loaded = sem("utok_made"), sem("acc_loaded")
        logits_ready, router_diff, router_exp = sem("logits_ready"), sem("router_diff"), sem("router_exp")
        logits_moved = sem("logits_moved")
        chosen, ranked, items_ready = sem("chosen"), sem("ranked"), sem("items_ready")
        selw_ready = sem("selw_ready")
        sel_ready, sel_turned, selT_ready = sem("sel_ready"), sem("sel_turned"), sem("selT_ready")
        x_gathered, xh_made, xl_made = sem("x_gathered"), sem("xh_made"), sem("xl_made")
        mhi_made, mlo_made, chunk_done = sem("mhi_made"), sem("mlo_made"), sem("chunk_done")
        sg_made, h_made, h_turned, hh_made, hl_made = (
            sem("sg_made"), sem("h_made"), sem("h_turned"), sem("hh_made"), sem("hl_made"))
        y_out, combined, acc_added, item_step = sem("y_out"), sem("combined"), sem("acc_added"), sem("item_step")
        out_stored = sem("out_stored")

        class Steps:

            def __init__(self, eng, s):
                self.eng, self.s, self.n = eng, s, 0

            def __call__(self, ins):
                ins.then_inc(self.s, 1)
                self.n += 1

            def wait(self):
                self.eng.wait_ge(self.s, self.n)

        def drained(eng, o):
            eng.wait_ge(bank_free[o % 2], o // 2 + 1)

        def tile_source(layer, kind, i):
            w = A["w_in"][layer].rearrange("(k p) c -> p k c", p=P)
            if kind in ("dq", "dkv", "kr", "gd", "gq", "gk", "r", "hg", "gate"):
                c0 = COL[kind] + (i * P if kind not in ("kr", "gd") else 0)
                return w[:, :, c0:c0 + P], (KD, P)
            if kind == "v":
                c0 = COL["gv"] + i * P if i < 4 else COL["hi"] + (i - 4) * P
                return w[:, :, c0:c0 + P], (KD, P)
            if kind in ("f", "q"):
                c0 = COL["hf" if kind == "f" else "hq"] + i * P
                return w[:, :, c0:c0 + P], (KD, P)
            if kind == "wo":
                wo = A[("w_mla_o", "w_gla_o", "w_hgrn_o")[i // 4]][layer].rearrange("(k p) c -> p k c", p=P)
                return wo[:, :, (i % 4) * 256:(i % 4 + 1) * 256], (4, 256)
            if kind == "wout":
                wo = A["w_out"][layer].rearrange("(k p) c -> p k c", p=P)
                return wo[:, :, i * P:(i + 1) * P], (KD, P)
            if kind in ("fg", "fu"):
                wf = A["w_ff_gate" if kind == "fg" else "w_ff_up"][layer // 2].rearrange("(k p) c -> p k c", p=P)
                return wf[:, :, i * P:(i + 1) * P], (KD, P)
            m, j = i // 3, i % 3
            wf = A["w_ff_down"][layer // 2].rearrange("(k p) c -> p k c", p=P)
            n = min(8, NF - 8 * j)
            return wf[:, 8 * j:8 * j + n, m * P:(m + 1) * P], (n, P)

        def expert_chunk(e, k):
            if k < 2 * N_GU:
                w = A["w_exp_gate" if k % 2 == 0 else "w_exp_up"]
                w = w.rearrange("l e (k p) c -> (l e) p k c", p=P)
                j = k // 2
                return w[bass.ds(e, 1), :, :, j * EC:(j + 1) * EC].rearrange("o p k c -> (o p) k c"), (KD, EC)
            w = A["w_exp_down"].rearrange("l e (k p) c -> (l e) p k c", p=P)
            j = k - 2 * N_GU
            return w[bass.ds(e, 1), :, 2 * j:2 * j + 2, :].rearrange("o p k c -> (o p) k c"), (2, D)

        last_out = of_job[-1]["out"]
        norm_before = {g for g, (_, k, i) in enumerate(jobs) if g and i == 0 and k in ("dq", "fg")}
        norm_after = {n + 1: of_job[g]["out"] - KD for n, g in enumerate(sorted(norm_before))}
        norm_after[len(norm_before) + 1] = last_out + 1 - KD
        squares_at = {}
        phase = 0
        for g, (_, kind, i) in enumerate(jobs):
            if kind == "wout" or kind == "fd" and i % 3 == 2:
                m = i if kind == "wout" else i // 3
                phase += m == 0
                if m < KD - 1:
                    squares_at[g + 1] = (phase, m)
        need_u = {g: n for n, g in enumerate(g for g, (_, k, i) in enumerate(jobs)
                                             if i == 0 and k in ("dq", "wout", "fg"))}
        block = ctx.enter_context(nc.Block())

        @block.sync
        def _(sp):
            sp.dma_start(vtok[0:META, 0:2, :], A["meta_tokens"].rearrange("t (k c) -> t k c", k=2)).then_inc(meta_landed, 16)
            sp.dma_start(C[:, 0:2 * P], A["consts"][:, 0:2 * P]).then_inc(meta_landed, 16)
            for half in range(2):
                f = slice(half * (D // 2), (half + 1) * (D // 2))
                sp.dma_start(x_in[:, :, f], A["x"][0, :, f].rearrange("(b p) d -> p b d", p=P)).then_inc(x_landed[half], 16)
            sp.dma_start(par[:], A["params"]).then_inc(par_landed, 16)
            for g, (layer, kind, i) in enumerate(jobs):
                if g == 2:
                    sp.dma_start(C[:, 2 * P:], A["consts"][:, 2 * P:]).then_inc(const_landed, 16)
                if kind == "gd":
                    if layer:
                        drained(sp, J(layer, "dq", 0)["out"] - 1)
                        drained(sp, J(layer, "dq", 0)["out"] - 2)
                    sp.dma_start(wuq[:], A["w_mla_uq"][layer].rearrange("(k p) c -> p k c", p=P)).then_inc(small_landed, 16)
                    sp.dma_start(wukv[:], A["w_mla_ukv"][layer]).then_inc(small_landed, 16)
                    sp.dma_start(wg2[:], A["w_gla_g2"][layer]).then_inc(small_landed, 16)
                if g >= RAW:
                    sp.wait_ge(stream_done, of_job[g - RAW]["part"] + of_job[g - RAW]["parts"])
                src, (r, c) = tile_source(layer, kind, i)
                sp.dma_start(raw[g % RAW][:, 0:r * c].rearrange("p (r c) -> p r c", r=r), src).then_inc(landed[g % RAW], 16)
            last_wo = J(DEPTH - 1, "wo", 3)
            sp.wait_ge(stream_done, last_wo["part"] + last_wo["parts"])
            sp.wait_ge(mix_done, 16 * DEPTH)
            sp.dma_start(MC[:], A["moe_consts"]).then_inc(moe_const, 16)
            sp.dma_start(wr[:], A["w_router"][0].rearrange("(k p) e -> p k e", p=P)).then_inc(moe_const, 16)
            sp.dma_start(brb[:], A["b_router"][0:1, :].broadcast_to([P, NE])).then_inc(moe_const, 16)

            def wait_slot(k, done):
                if k != 2 * N_GU:
                    sp.wait_ge(chunk_done, done + (k == 2 * N_GU - 1))

            def load_chunk(e, k):
                src, (r, c) = expert_chunk(e, k)
                sp.dma_start(mraw[k % MRAW][:].rearrange("p (r c) -> p r c", r=r), src).then_inc(mlanded[k % MRAW], 16)

            for k in range(MRAW):
                load_chunk(0, k)
            sp.wait_ge(items_ready, 2)
            n_items = sp.value_load(nit_i[0:1, 0:1], min_val=1, max_val=12)
            n_before = sp.value_load(nit_i[0:1, 1:2], min_val=0, max_val=11)
            with sp.Fori(0, n_before) as i:
                e = sp.value_load(it_i[0:1, bass.ds(i, 1)], min_val=0, max_val=NE - 1)
                for k in range(MRAW, ITEM):
                    wait_slot(k, i * ITEM + (k - MRAW + 1))
                    load_chunk(e, k)
                e = sp.value_load(it_i[0:1, bass.ds(i + 1, 1)], min_val=0, max_val=NE - 1)
                for k in range(MRAW):
                    wait_slot(k, i * ITEM + (ITEM + k - MRAW + 1))
                    load_chunk(e, k)
            e = sp.value_load(it_i[0:1, bass.ds(n_before, 1)], min_val=0, max_val=NE - 1)
            for k in range(MRAW, ITEM):
                wait_slot(k, n_before * ITEM + (k - MRAW + 1))
                load_chunk(e, k)
            for q in range(4):
                sp.wait_ge(acc_added, n_items * 4 + (q + 1))
                b, f = q // 2, slice((q % 2) * 512, (q % 2 + 1) * 512)
                sp.dma_start(out[0, b * P:(b + 1) * P, f], acc[:, b, f]).then_inc(out_stored, 16)
            sp.wait_ge(out_stored, 64)

        @block.gpsimd
        def _(pool):
            for layer, kind, i in jobs:
                if kind == "wo" and ORDER[i // 4] > 0:
                    for half in range(2):
                        b, m = i // 4, 2 * (i % 4) + half
                        o = J(layer, kind, i)["out"] + half
                        drained(pool, o)
                        drained(pool, J(layer, "wo", 4 + i % 4)["out"] + half)
                        if ORDER[b] == 2:
                            pool.wait_ge(mix_done, mixed_by(layer, 2, m))
                        c = live(layer, kind)
                        pool.tensor_tensor(mixed[:, m, c], mixed[:, m, c], gate_of(b, m)[:, c], ALU.add).then_inc(mix_done, 1)
            pool.wait_ge(norm_r, len(norm_before) + 2)
            pool.memset(ys[:], 0.0)
            pool.memset(selT[:], 0.0).then_inc(zeroed, 1)
            pool.wait_ge(items_ready, 2)
            n_before = pool.value_load(nit_i[0:1, 1:2], min_val=0, max_val=11)
            for k in range(MLOOK - 1):
                pool.wait_ge(chunk_done, n_before * ITEM + (ITEM + k - MRAW + 1))
                pool.memset(mraw[k % MRAW][:], 0.0).then_inc(mlanded[k % MRAW], 16)

        @block.scalar
        def _(act):
            st = Steps(act, act_step)
            A_ = nc.scalar.activation

            def split_hi(g):
                layer, kind, i = jobs[g]
                n = tile_source(layer, kind, i)[1]
                n = n[0] * n[1]
                act.wait_ge(landed[g % RAW], 16 * (g // RAW + 1))
                if g >= HI:
                    act.wait_ge(stream_done, of_job[g - HI]["part"] + of_job[g - HI]["parts"])
                A_(hi[g % HI][:, 0:n], raw[g % RAW][:, 0:n], ACT.Copy).then_inc(hi_made, 1)

            def square(phase, m):
                if phase == 0:
                    act.wait_ge(h_loaded, m + 1)
                else:
                    drained(act, norm_after[phase] + m)
                A_(gt[:, m, :], hT[:, m, :], ACT.Square).then_inc(norm_sq, 1)

            def norm(phase, split=True):
                if phase:
                    square(phase, KD - 1)
                act.wait_ge(norm_sum, phase + 1)
                st(A_(rr[:], bank[2][:, 0:T], ACT.Ln, bias=eps[:, 0:1], scale=1.0 / D))
                st.wait()
                A_(rr[:], rr[:], ACT.Exp, scale=-0.5).then_inc(norm_r, 1)
                for k in range(KD if split else 0):
                    act.wait_ge(u_whole, KD * phase + k + 1)
                    A_(UH[:, k, :], mixed[:, k, :], ACT.Copy).then_inc(u_hi, 1)

            def sigmoid(x, ps, made, read):
                A_(x, ps, ACT.Relu, bias=guard[:, 0:1]).then_inc(read[0], 1)
                act.wait_ge(*read)
                st(A_(x, x, ACT.Exp, bias=guard[:, 0:1], scale=-1.0))
                st.wait()
                st(A_(x, x, ACT.Ln, bias=1.0))
                st.wait()
                A_(x, x, ACT.Exp, scale=-1.0).then_inc(made, 1)

            def evacuate(g):
                layer, kind, i = jobs[g]
                j = of_job[g]
                o = j["out"]
                if kind in ("gk", "wo", "wout", "fd", "fu"):
                    return
                c = live(layer, kind)
                ps = bank[o % 2][:, c]
                free = bank_free[o % 2]
                act.wait_ge(stream_done, j["part"] + 1)
                if kind in ("dq", "dkv"):
                    t = i if kind == "dq" else 2
                    st(A_(dqT[:, t, :], ps, ACT.Copy))
                    A_(gt[:, t, :], ps, ACT.Square).then_inc(free, 1)
                elif kind == "kr":
                    st(A_(qk[NOPE:QK, 0, 1, :], ps[NOPE:QK], ACT.Copy))
                    A_(qk[NOPE:QK, 1, 1, :], ps[NOPE:QK], ACT.Copy).then_inc(free, 1)
                elif kind == "gq":
                    A_(Q[:, i, OFF:LP], ps, ACT.Copy, scale=GLA_DK ** -0.5).then_inc(free, 1)
                elif kind == "gd":
                    A_(gdT[:], ps[0:16], ACT.Copy).then_inc(free, 1)
                elif kind == "v":
                    A_(VT[:, i if i < 4 else (i - 4) % 2, :], ps, ACT.Copy).then_inc(free, 1)
                elif kind == "f":
                    sigmoid(X[:, i % 2, OFF:LP], ps, f_sig, (free, o // 2 + 1))
                elif kind in ("q", "r", "hg", "fg"):
                    if j["silu"] >= 2:
                        act.wait_ge(silu_done, j["silu"] - 1)
                    x = ez[:, j["silu"] % 2, c]
                    if kind == "fg":
                        A_(x, ps, ACT.Silu).then_inc(free, 1)
                    else:
                        sigmoid(x, ps, exp_made, (logit_read, j["exp"] + 1))
                elif kind == "gate":
                    b, m = divmod(i, 8)
                    if b == 0:
                        act.wait_ge(silu_done, J(layer, "r" if m < 4 else "hg", m % 4)["silu"] + 1)
                    elif b == 2 and m < 5:
                        act.wait_ge(mla_dve, N(layer, "ss", 0, "dve"))
                    sigmoid(gate_of(b, m)[:, c], ps, gate_made, (free, o // 2 + 1))

            def mixture_hi(g):
                layer, kind, i = jobs[g]
                if kind == "wo" and ORDER[i // 4] == 2:
                    for m in (2 * i, 2 * i + 1):
                        act.wait_ge(mix_done, mixed_by(layer, 0, m))
                        c = live(layer, kind)
                        A_(UH[:, m, c], mixed[:, m, c], ACT.Copy).then_inc(mixed_hi, 1)

            def mla(layer, name, i):
                p = i % 2
                Ma, Mb = bank[2 + 2 * p], bank[3 + 2 * p]
                act.wait_ge(mla_psum, N(layer, name, i, "pe"))
                if name == "ss":
                    st(A_(rin[:, 0, :], bank[2][:, 0:T], ACT.Ln, bias=eps[:, 0:1], scale=1.0 / 256))
                    st(A_(rin[:, 1, :], bank[3][:, 0:T], ACT.Ln, bias=eps[:, 0:1], scale=1.0 / 128))
                    st.wait()
                    A_(rin, rin, ACT.Exp, scale=-0.5).then_inc(mla_act, 1)
                elif name == "vm":
                    st(A_(vtok[0:META, 0, :], bank[4][0:META, :], ACT.Copy))
                    st(A_(vtok[:, 1, :], bank[5][:], ACT.Copy))
                    A_(vtok[:, 2, :], bank[2][:], ACT.Copy).then_inc(mla_act, 1)
                elif name == "qk":
                    if i >= 2:
                        act.wait_ge(mla_psum, N(layer, "sc", i - 2, "pe"))
                    st(A_(qk[:, p, 0, :], Ma[0:QK, 0:T], ACT.Copy))
                    A_(qsq[:, p, 0, :], Ma[0:QK, 0:T], ACT.Square).then_inc(mla_act, 1)
                elif name == "nrm":
                    st(A_(qsq[:, p, 0, :], Ma[0:QK, 0:T], ACT.Ln, bias=eps[0:QK, 0:1], scale=1.0 / QK))
                    st(A_(qsq[:, p, 1, :], Mb[0:QK, 0:T], ACT.Ln, bias=eps[0:QK, 0:1], scale=1.0 / QK))
                    st.wait()
                    A_(qsq[:, p, :, :], qsq[:, p, :, :], ACT.Exp, scale=-0.5).then_inc(mla_act, 1)
                elif name == "sc":
                    act.wait_ge(mla_dve, N(layer, "sc", i, "dve"))
                    st(A_(pr[:, p, 0:272], pr[:, p, 0:272], ACT.Exp, bias=mx[:, p, 0:1], accum_out=sm[:, p, 0:1]))
                    st(A_(pr[:, p, 272:416], pr[:, p, 272:416], ACT.Exp, bias=mx[:, p, 1:2], accum_out=sm[:, p, 1:2]))
                    A_(pr[0:META, p, 416:432], pr[0:META, p, 416:432], ACT.Exp, bias=mx[0:META, p, 2:3],
                       accum_out=sm[0:META, p, 2:3]).then_inc(mla_act, 1)
                elif name == "pt":
                    A_(ptf[:, p, :], Mb[:, 0:384], ACT.Copy).then_inc(mla_act, 1)
                elif name == "ot":
                    act.wait_ge(stream_done, J(layer, "wo", 11)["part"] + 2)
                    A_(OH[:, i, :], bank[2 + i][:, 0:T], ACT.Copy).then_inc(mla_act, 1)

            def la(unit, name, i):
                scale = 1.0 / 16 if unit % 3 == 0 else 1.0
                layer = unit // 3
                L = bank[6 + i % 2]
                if name == "gz":
                    act.wait_ge(la_psum, N(unit, name, i, "pe"))
                    for t in range(2):
                        st(A_(X[:, t, OFF:LP], bank[6 + t][:, 0:T], ACT.Abs,
                              bias=par[:, layer, PCOL["bg"] + t:PCOL["bg"] + t + 1]))
                    st.wait()
                    st(A_(X[:, :, OFF:LP], X[:, :, OFF:LP], ACT.Exp, scale=-1.0))
                    st.wait()
                    A_(X[:, :, OFF:LP], X[:, :, OFF:LP], ACT.Ln, bias=1.0).then_inc(la_act, 1)
                elif name == "pre":
                    act.wait_ge(f_ready, 4 * layer + 2 * (unit % 3))
                    A_(G[:, :, OFF:LP], X[:, :, OFF:LP], ACT.Ln).then_inc(la_act, 1)
                elif name == "scan":
                    act.wait_ge(la_dve, N(unit, "scan", 0, "dve"))
                    st(A_(QE[:], X[:], ACT.Exp, scale=scale))
                    A_(KE[:], X[:], ACT.Exp, scale=-scale).then_inc(la_act, 1)
                elif name == "mul1":
                    act.wait_ge(la_act, N(unit, "scan", 0, "act"))
                    A_(X[:], B[:], ACT.Exp, scale=scale).then_inc(la_act, 1)
                elif name == "mul2":
                    act.wait_ge(la_dve, N(unit, "mul2", 0, "dve"))
                    st(A_(dec[:], B[:].rearrange("p t (c j) -> p t c j", j=CH)[:, :, :, CH - 1], ACT.Exp, scale=scale))
                    A_(X[:], X[:], ACT.Exp, scale=scale).then_inc(la_act, 1)
                elif name == "vt":
                    act.wait_ge(la_psum, N(unit, name, i, "pe"))
                    rows, w = (META if i == 0 else CH), heads_of(unit) * P
                    A_(V[0:rows, i, 0:w], L[0:rows, 0:w], ACT.Copy).then_inc(la_act, 1)
                elif name == "o":
                    act.wait_ge(la_psum, N(unit, name, i, "pe"))
                    if (unit, i) != (0, 0) and (unit, i) != (0, 1):
                        before = (unit, "n", i - 2) if i >= 2 else (unit - 1, "n", heads_of(unit - 1) - 2 + i)
                        act.wait_ge(la_dve, N(*before, "dve"))
                    st(A_(ob[:, i % 2, :], L[:, 0:T], ACT.Copy))
                    A_(osq[:, i % 2, :], L[:, 0:T], ACT.Square).then_inc(la_act, 1)
                elif name == "n":
                    act.wait_ge(la_psum, N(unit, name, i, "pe"))
                    st(A_(rl[:, i % 2, :], L[:, 0:T], ACT.Ln, bias=eps[:, 0:1], scale=1.0 / P))
                    st.wait()
                    A_(rl[:, i % 2, :], rl[:, i % 2, :], ACT.Exp, scale=-0.5).then_inc(la_act, 1)

            act.preload_act_table_set("natural_log_exp_and_others")
            for m in range(KD):
                square(0, m)
            for g in range(LOOK):
                split_hi(g)
            norm(0)
            act.wait_ge(lb_sub, 1)
            A_(lbt[:, 1:3, :], lbt[:, 1:3, :], ACT.Exp).then_inc(lb_exp, 1)
            phase = 1
            for g in range(NG):
                if g + LOOK < NG:
                    split_hi(g + LOOK)
                if g in norm_before:
                    if jobs[g][1] == "dq":
                        act.preload_act_table_set("natural_log_exp_and_others")
                    norm(phase)
                    phase += 1
                for half in range(2):
                    if half == 0 and g:
                        mixture_hi(g - 1)
                    if half == 0 and g in squares_at:
                        square(*squares_at[g])
                    if half == 1:
                        evacuate(g)
                    for s in shares["act"].get(2 * g + half, ()):
                        if s[1] in ACT_PART:
                            (mla if s[1] in MLA_NAMES else la)(*s)

            norm(phase, False)

            def expert_hi(k, landings):
                act.wait_ge(mlanded[k % MRAW], landings)
                A_(mhi[k % MHI][:], mraw[k % MRAW][:], ACT.Copy).then_inc(mhi_made, 1)

            def gathered_hi(first):
                for half in range(2):
                    act.wait_ge(x_gathered, first + half)
                    A_(xh[:, 4 * half:4 * half + 4, :].rearrange("p k s -> p (k s)"), bank[4 + half][:],
                       ACT.Copy).then_inc(xh_made, 1)

            for k in range(2):
                expert_hi(k, 16)
            for b in range(2):
                for half in range(2):
                    for n, (made, turned, to) in enumerate(((utok_made, turned_u, utok), (acc_loaded, turned_h, acc))):
                        act.wait_ge(turned, 2 * b + half + 1)
                        A_(to[:, b, half * 512:(half + 1) * 512], bank[2 * n + half][:], ACT.Copy).then_inc(made, 1)
            act.wait_ge(router_diff, 1)
            A_(top[:, :, 2], top[:, :, 2], ACT.Exp).then_inc(router_exp, 1)
            for k in range(2, MLOOK - 1):
                expert_hi(k, 16)
            act.wait_ge(items_ready, 2)
            n_items = act.value_load(nit_i[0:1, 0:1], min_val=1, max_val=12)

            act.sem_inc(y_out, 2)
            gathered_hi(1)
            with act.Fori(0, n_items) as i:
                expert_hi(MLOOK - 1, i * (ITEM // MRAW) * 16 + 16)
                for k in range(ITEM):
                    act.wait_ge(chunk_done, i * ITEM + (k + 1))
                    if k % 2 == 1 and k < 2 * N_GU:
                        j = k // 2
                        act.wait_ge(h_made, i * N_GU + (j + 1))
                        A_(sg[:, j % 2, :], bank[j % 2][:, 0:EC], ACT.Silu).then_inc(sg_made, 1)
                    if k % 2 == 0 and 4 <= k <= 2 * N_GU + 2:
                        j = (k - 4) // 2
                        act.wait_ge(h_turned, i * N_GU + (j + 1))
                        A_(hh[:, 2 * j:2 * j + 2, :].rearrange("p f s -> p (f s)"), bank[6 + j % 2][:, 0:2 * P],
                           ACT.Copy).then_inc(hh_made, 1)
                    if k == GATHER_AT + 1:
                        gathered_hi(i * 2 + 3)
                    if k == ITEM - 1:
                        for half in range(2):
                            A_(ys[:, half * 512:(half + 1) * 512], bank[2 + half][:], ACT.Copy).then_inc(y_out, 1)
                    if k < ITEM - 1:
                        n = k + MLOOK
                        expert_hi(n % ITEM, (i * (ITEM // MRAW) + (n // MRAW + 1)) * 16)

        @block.vector
        def _(dve):
            st = Steps(dve, dve_step)
            E = nc.vector
            TT, TS, STT, CP = E.tensor_tensor, E.tensor_scalar, E.scalar_tensor_tensor, E.tensor_copy

            def split_lo(g):
                layer, kind, i = jobs[g]
                n = tile_source(layer, kind, i)[1]
                n = n[0] * n[1]
                dve.wait_ge(hi_made, g + 1)
                TT(lo[g % RAW][:, 0:n], raw[g % RAW][:, 0:n], hi[g % HI][:, 0:n].bitcast(F32),
                   ALU.subtract).then_inc(lo_made, 1)

            def norm(phase, gain, split):
                dve.wait_ge(norm_r, phase + 1)
                for k in range(KD + 2 if split else KD):
                    if k < KD:
                        STT(mixed[:, k, :], hT[:, k, :], gain[:, k:k + 1], rr[:], ALU.mult, ALU.mult).then_inc(u_whole, 1)
                    if split and k >= 2:
                        m = k - 2
                        dve.wait_ge(u_hi, KD * phase + m + 1)
                        TT(UL[:, m, :], mixed[:, m, :], UH[:, m, :].bitcast(F32), ALU.subtract).then_inc(u_ready, 1)

            def polish(roots):
                for r, a, x, n in roots:
                    st(STT(a, r, -0.5 / n, r, ALU.mult, ALU.mult))
                st.wait()
                for r, a, x, n in roots:
                    st(STT(a, x, EPS * n, a, ALU.add, ALU.mult))
                st.wait()
                for r, a, x, n in roots:
                    st(STT(r, a, 1.5, r, ALU.add, ALU.mult))
                st.wait()

            def zero_pads():
                for t in (Q, K, G):
                    st(E.memset(t[:, :, 0:OFF], 0.0))
                st(E.memset(AT[:], 0.0))

            def evacuate(g):
                layer, kind, i = jobs[g]
                j = of_job[g]
                o = j["out"]
                if kind in ("dq", "dkv", "kr", "gq", "gd", "v", "f", "gate", "fg") or kind == "fd" and i % 3 < 2:
                    return
                c = live(layer, kind)
                ps = bank[o % 2][:, c]
                free = bank_free[o % 2]
                if kind == "gk":
                    dve.wait_ge(stream_done, j["part"] + 1)
                    CP(K[:, i, OFF:LP], ps).then_inc(free, 1)
                elif kind == "q":
                    dve.wait_ge(logit_read, j["exp"] + 1)
                    CP(Q[:, i % 2, OFF:LP], ps).then_inc(free, 1)
                elif kind in ("r", "hg"):
                    dve.wait_ge(logit_read, j["exp"] + 1)
                    x = O[:, 0 if kind == "r" else 1, i, c]
                    u, h = (0, i) if kind == "r" else (1 + i // 2, i % 2)
                    dve.wait_ge(la_dve, N(3 * layer + u, "n", h, "dve"))
                    TT(x, x, ps, ALU.mult).then_inc(free, 1)
                elif kind == "wo":
                    b = i // 4
                    for half in range(2):
                        m = 2 * (i % 4) + half
                        oo = o + half
                        dve.wait_ge(stream_done, j["part"] + half + 1)
                        dve.wait_ge(gate_made, J(layer, "gate", 8 * b + m)["gate"] + 1)
                        x = gate_of(b, m)[:, c]
                        TT(x, x, bank[oo % 2][:, c], ALU.mult).then_inc(bank_free[oo % 2], 1)
                elif kind in ("wout", "fd"):
                    m = i if kind == "wout" else i // 3
                    dve.wait_ge(stream_done, j["part"] + 1)
                    TT(hT[:, m, c], hT[:, m, c], ps, ALU.add).then_inc(free, 1)
                elif kind == "fu":
                    dve.wait_ge(stream_done, j["part"] + 1)
                    drained(dve, o - 1)
                    x = ez[:, j["silu"] % 2, :]
                    TT(x, x, ps, ALU.mult).then_inc(free, 1)
                    drained(dve, o)
                    st(CP(HH[:, i, :], x))
                    st.wait()
                    TT(HL[:, i, :], x, HH[:, i, :].bitcast(F32), ALU.subtract).then_inc(silu_done, 1)

            def finish(g):
                layer, kind, i = jobs[g]
                j = of_job[g]
                o = j["out"]
                c = live(layer, kind)
                if kind == "wo" and ORDER[i // 4] == 2:
                    for m in (2 * i, 2 * i + 1):
                        dve.wait_ge(mixed_hi, KD * layer + m + 1)
                        TT(UL[:, m, c], mixed[:, m, c], UH[:, m, c].bitcast(F32), ALU.subtract).then_inc(u_ready, 1)
                if kind == "f":
                    t = i % 2
                    dve.wait_ge(f_sig, 4 * layer + i + 1)
                    if layer == 0 and i == 0:
                        dve.wait_ge(lb_ready, 1)
                    x = X[:, t, OFF:LP]
                    st(TS(x, x, lbp[:, layer, 1, i:i + 1], lbp[:, layer, 0, i:i + 1], ALU.mult, ALU.add))
                    st.wait()
                    TS(K[:, t, OFF:LP], x, -1.0, 1.0, ALU.mult, ALU.add).then_inc(f_ready, 1)
                elif kind == "q":
                    dve.wait_ge(exp_made, j["exp"] + 1)
                    drained(dve, o)
                    x = Q[:, i % 2, OFF:LP]
                    TT(x, ez[:, j["silu"] % 2, :], x, ALU.mult).then_inc(silu_done, 1)
                elif kind in ("r", "hg"):
                    dve.wait_ge(exp_made, j["exp"] + 1)
                    drained(dve, o)
                    x = ez[:, j["silu"] % 2, c]
                    st(TT(x, x, O[:, 0 if kind == "r" else 1, i, c], ALU.mult))
                    st.wait()
                    if i == 0 and kind == "hg":
                        dve.wait_ge(stream_done, J(layer, "wo", 7)["part"] + 2)
                    st(CP(OH[:, i, c], x))
                    st.wait()
                    TT(OL[:, i, c], x, OH[:, i, c].bitcast(F32), ALU.subtract).then_inc(silu_done, 1)

            def mla(layer, name, i):
                p = i % 2
                Ma, Mb = bank[2 + 2 * p], bank[3 + 2 * p]
                gain = lambda n, rows=P: par[0:rows, layer, PCOL[n]:PCOL[n] + 1]
                if name == "ss":
                    dve.wait_ge(mla_act, N(layer, name, i, "act"))
                    for t in range(3):
                        g = par[:, layer, PCOL["cq"] + t:PCOL["cq"] + t + 1] if t < 2 else gain("ckv")
                        ins = STT(dqT[:, t, :], dqT[:, t, :], g, rin[:, t // 2, :], ALU.mult, ALU.mult)
                        if t < 2:
                            st(ins)
                        else:
                            ins.then_inc(mla_dve, 1)
                elif name == "qk":
                    dve.wait_ge(mla_psum, N(layer, name, i, "pe"))
                    if i >= 2:
                        dve.wait_ge(mla_act, N(layer, name, i, "act"))
                        st(CP(qk[NOPE:QK, p, 1, :], kr_keep[NOPE:QK, :]))
                    else:
                        st(CP(kr_keep[NOPE:QK, :], qk[NOPE:QK, p, 1, :]))
                    st(CP(qk[0:NOPE, p, 1, :], Mb[0:NOPE, 0:T]))
                    st.wait()
                    TT(qsq[:, p, 1, :], qk[:, p, 1, :], qk[:, p, 1, :], ALU.mult).then_inc(mla_dve, 1)
                elif name == "nrm":
                    dve.wait_ge(mla_act, N(layer, name, i, "act"))
                    polish([(qsq[:, p, 0, :], pr[0:QK, p, 0:T], Ma[0:QK, 0:T], QK),
                            (qsq[:, p, 1, :], ptf[0:QK, p, 0:T], Mb[0:QK, 0:T], QK)])
                    st(STT(qk[:, p, 0, :], qk[:, p, 0, :], gain("qn", QK), qsq[:, p, 0, :], ALU.mult, ALU.mult))
                    STT(qk[:, p, 1, :], qk[:, p, 1, :], gain("kn", QK), qsq[:, p, 1, :],
                        ALU.mult, ALU.mult).then_inc(mla_dve, 1)
                elif name == "rot":
                    dve.wait_ge(mla_psum, N(layer, name, i, "pe"))
                    cos, sin = C[NOPE:QK, cc["cos"]], C[NOPE:QK, cc["sin"]]
                    for t, M in ((0, Ma), (1, Mb)):
                        st(TT(qsq[NOPE:QK, p, t, :], sin, M[NOPE:QK, 0:T], ALU.mult))
                        st(TT(qk[NOPE:QK, p, t, :], qk[NOPE:QK, p, t, :], cos, ALU.mult))
                    st.wait()
                    TT(qk[NOPE:QK, p, :, :], qk[NOPE:QK, p, :, :], qsq[NOPE:QK, p, :, :], ALU.add).then_inc(mla_dve, 1)
                elif name == "sc":
                    dve.wait_ge(mla_psum, N(layer, name, i, "pe"))
                    if (layer, i) not in ((0, 0), (0, 1)):
                        before = (layer, "pt", i - 2) if i >= 2 else (layer - 1, "pt", HEADS - 2 + i)
                        dve.wait_ge(mla_psum, N(*before, "pe"))
                    mask = C[:, cc["smask"]]
                    st(STT(pr[:, p, 0:416], Ma[:, 0:416], QK ** -0.5, mask[:, 0:416], ALU.mult, ALU.add))
                    st(STT(pr[0:META, p, 416:432], Ma[0:META, 416:432], QK ** -0.5, mask[0:META, 416:432],
                           ALU.mult, ALU.add))
                    st.wait()
                    st(E.tensor_reduce(mx[:, p, 0:1], pr[:, p, 0:272], AX.X, ALU.max, negate=True))
                    st(E.tensor_reduce(mx[:, p, 1:2], pr[:, p, 272:416], AX.X, ALU.max, negate=True))
                    E.tensor_reduce(mx[0:META, p, 2:3], pr[0:META, p, 416:432], AX.X, ALU.max,
                                    negate=True).then_inc(mla_dve, 1)
                elif name == "pt":
                    dve.wait_ge(mla_psum, N(layer, name, i, "pe"))
                    st(E.reciprocal(sm[:, p, 0:2], sm[:, p, 0:2]))
                    st(E.reciprocal(sm[0:META, p, 2:3], sm[0:META, p, 2:3]))
                    st(CP(ptm[:, p, 0:256], Ma[0:META, 0:256]))
                    CP(ptm[:, p, 256:272], Ma[0:META, 256:272]).then_inc(mla_dve, 1)
                elif name == "pv":
                    dve.wait_ge(mla_psum, N(layer, name, i, "pe"))
                    dve.wait_ge(mla_dve, N(layer, "pt", i, "dve"))
                    c = slice(i * VDIM, (i + 1) * VDIM)
                    st(TS(otok[:, 2, c], Ma[:, 0:VDIM], sm[:, p, 0:1], None, ALU.mult))
                    st(TS(otok[:, 1, c], Mb[:, 0:VDIM], sm[:, p, 1:2], None, ALU.mult))
                    TS(otok[0:META, 0, c], Mb[0:META, VDIM:2 * VDIM], sm[0:META, p, 2:3], None,
                       ALU.mult).then_inc(mla_dve, 1)
                elif name == "ot":
                    dve.wait_ge(mla_act, N(layer, name, i, "act"))
                    TT(OL[:, i, :], bank[2 + i][:, 0:T], OH[:, i, :].bitcast(F32), ALU.subtract).then_inc(mla_dve, 1)

            def la(unit, name, i):
                layer, u = divmod(unit, 3)
                L = bank[6 + i % 2]
                chunks = lambda t: t[:].rearrange("p t (c j) -> p (t c) j", j=CH)
                if name == "gz":
                    dve.wait_ge(la_act, N(unit, name, i, "act"))
                    for t in range(2):
                        st(TS(G[:, t, OFF:LP], bank[6 + t][:, 0:T], par[:, layer, PCOL["bg"] + t:PCOL["bg"] + t + 1],
                              0.0, ALU.add, ALU.min))
                    st.wait()
                    TT(G[:, :, OFF:LP], G[:, :, OFF:LP], X[:, :, OFF:LP], ALU.subtract).then_inc(la_dve, 1)
                elif name == "scan":
                    if u == 0:
                        dve.wait_ge(la_dve, N(unit, "gz", 0, "dve"))
                        st(E.memset(S[:], 0.0))
                    else:
                        dve.wait_ge(la_act, N(unit, "pre", 0, "act"))
                    for t in range(2):
                        st(E.tensor_tensor_scan(B[:, t, :], C[:, cc["reset"]], G[:, t, :], 0.0, ALU.mult, ALU.add))
                    st.wait()
                    ref = chunks(B)[:, :, CH // 2 - 1:CH // 2].broadcast_to([P, 2 * NCH, CH])
                    TT(chunks(X), chunks(B), ref, ALU.subtract).then_inc(la_dve, 1)
                elif name == "mul1":
                    dve.wait_ge(la_act, N(unit, "scan", 0, "act"))
                    if u:
                        dve.wait_ge(silu_done, J(layer, "q", 2 * u - 1)["silu"] + 1)
                    else:
                        drained(dve, J(layer, "gk", 1)["out"])
                        drained(dve, J(layer, "gk", 0)["out"])
                    st(TT(QE[:], QE[:], Q[:], ALU.mult))
                    st(TT(KE[:], KE[:], K[:], ALU.mult))
                    dve.wait_ge(la_act, N(unit, "mul1", 0, "act"))
                    st.wait()
                    TT(Q[:], Q[:], X[:], ALU.mult).then_inc(la_dve, 1)
                elif name == "mul2":
                    dve.wait_ge(la_dve, N(unit, "mul1", 0, "dve"))
                    end = chunks(B)[:, :, CH - 1:CH].broadcast_to([P, 2 * NCH, CH])
                    TT(chunks(X), end, chunks(B), ALU.subtract).then_inc(la_dve, 1)
                elif name == "mul3":
                    dve.wait_ge(la_act, N(unit, "mul2", 0, "act"))
                    TT(K[:], K[:], X[:], ALU.mult).then_inc(la_dve, 1)
                elif name == "kt":
                    dve.wait_ge(la_psum, N(unit, name, i, "pe"))
                    if i == 0:
                        st(CP(KLT[0:META, 0, :], L[0:META, 0:256]))
                        CP(KLT[:, 1, :], L[0:CH, 256:512]).then_inc(la_dve, 1)
                    else:
                        CP(KLT[:, 2:4, :].rearrange("p c d -> p (c d)"), L[0:CH, :]).then_inc(la_dve, 1)
                elif name == "ds":
                    dve.wait_ge(la_psum, N(unit, name, i, "pe"))
                    where = [(2 * i, 0, 64), (2 * i + 1, 64, 128)] if u == 0 else [(i, 0, 128)]
                    for c in range(4):
                        for n, (h, a, b) in enumerate(where):
                            ps = L[a:b, c * P:(c + 1) * P]
                            if c == 0:
                                st(CP(S[a:b, 0, h, :], ps))
                            else:
                                ins = STT(S[a:b, c, h, :], S[a:b, c - 1, h, :], dec[a:b, i, c:c + 1], ps,
                                          ALU.mult, ALU.add)
                                if c == 3 and n == len(where) - 1:
                                    ins.then_inc(la_dve, 1)
                                else:
                                    st(ins)
                        if c < 3:
                            st.wait()
                elif name == "a":
                    dve.wait_ge(la_psum, N(unit, name, i, "pe"))
                    m = C[0:CH, cc["cos"]].bitcast(I32)
                    st(E.copy_predicated(AT[:, i % 2, 0:256], m[:, 0:256], L[0:CH, 0:256]))
                    E.copy_predicated(AT[0:META, i % 2, 256:272], m[0:META, 256:272],
                                      L[0:META, 256:272]).then_inc(la_dve, 1)
                elif name == "n":
                    dve.wait_ge(la_act, N(unit, name, i, "act"))
                    g = par[:, layer, PCOL["glao" if u == 0 else "hgrno"]:][:, 0:1]
                    where = O[:, 0, i, :] if u == 0 else O[:, 1, 2 * (u - 1) + i, :]
                    STT(where, ob[:, i % 2, :], g, rl[:, i % 2, :], ALU.mult, ALU.mult).then_inc(la_dve, 1)

            st(E.memset(guard[:], GUARD))
            E.memset(eps[:], EPS).then_inc(zeroed, 1)
            zero_pads()
            for k in range(KD):
                dve.wait_ge(x_turned, k + 1)
                CP(hT[:, k, :], bank[2 + k % 2][:, 0:T]).then_inc(h_loaded, 1)
            for g in range(LOOK_LO):
                split_lo(g)
            gains = [par[:, l, PCOL[n]:PCOL[n] + 8] for l in range(2) for n in ("attn", "ffn")]
            dve.wait_ge(par_landed, 16)
            norm(0, gains[0], True)
            l0, l1 = (par[:, l, PCOL["lb"]:PCOL["lb"] + 4] for l in range(2))
            st(TT(lbt[:, 0, :], l0, l1, ALU.max))
            st.wait()
            st(TT(lbt[:, 1, :], l0, lbt[:, 0, :], ALU.subtract))
            TT(lbt[:, 2, :], l1, lbt[:, 0, :], ALU.subtract).then_inc(lb_sub, 1)
            dve.wait_ge(lb_exp, 1)
            st(TT(lbt[:, 3, :], lbt[:, 1, :], lbt[:, 2, :], ALU.add))
            st.wait()
            st(E.reciprocal(lbt[:, 3, :], lbt[:, 3, :]))
            st.wait()
            for l in range(2):
                st(TT(lbt[:, 1 + l, :], lbt[:, 1 + l, :], lbt[:, 3, :], ALU.mult))
            st.wait()
            st(TT(lbt[:, 3, :], lbt[:, 1, :], lbt[:, 2, :], ALU.add))
            st(TT(lbp[:, 0, 0, :], lbt[:, 1, :], lbt[:, 1, :], ALU.subtract))
            st.wait()
            st(TT(lbp[:, 1, 0, :], lbt[:, 3, :], lbt[:, 1, :], ALU.subtract))
            st.wait()
            TS(lbp[:, :, 1, :], lbp[:, :, 0, :], -1.0, 1.0, ALU.mult, ALU.add).then_inc(lb_ready, 1)
            phase = 1
            for g in range(NG):
                if g + LOOK_LO < NG:
                    split_lo(g + LOOK_LO)
                if g in norm_before:
                    norm(phase, gains[phase], True)
                    if jobs[g][1] == "dq":
                        zero_pads()
                    phase += 1
                for half in range(2):
                    if half == 1:
                        evacuate(g)
                    elif g:
                        finish(g - 1)
                    for s in shares["dve"].get(2 * g + half, ()):
                        if s[1] in DVE_PART:
                            (mla if s[1] in MLA_NAMES else la)(*s)

            norm(phase, gains[phase], False)

            def expert_lo(k, made):
                dve.wait_ge(mhi_made, made)
                TT(mlo[k % MRAW][:], mraw[k % MRAW][:], mhi[k % MHI][:].bitcast(F32),
                   ALU.subtract).then_inc(mlo_made, 1)

            dve.wait_ge(logits_ready, 1)
            lgT = oh[0:NE].rearrange("p b t -> p (b t)")
            CP(lgT, bank[4][0:NE, 0:SEQ]).then_inc(logits_moved, 1)
            dve.wait_ge(logits_ready, 2)
            dve.wait_ge(moe_const, 48)
            R = lambda n: rt[:, n, :, :]
            lg, e1, s1, lg2, e2, s2, cs, gs, tmp = (R(n) for n in range(9))
            for b in range(2):
                st(TT(lg[:, b, :], brb[:], bank[5][:, 32 + 8 * b:40 + 8 * b], ALU.add))
            st.wait()

            def pick_first(which, values, eq, sel):
                st(E.tensor_reduce(top[:, :, which:which + 1], values, AX.X, ALU.max))
                st.wait()
                st(TT(eq, values, top[:, :, which:which + 1].broadcast_to([P, 2, NE]), ALU.is_equal))
                st.wait()
                for b in range(2):
                    st(E.tensor_tensor_scan(tmp[:, b, :], eq[:, b, :], eq[:, b, :], 0.0, ALU.add, ALU.bypass))
                st.wait()
                st(STT(sel, tmp, 1.0, eq, ALU.is_equal, ALU.mult))
                st.wait()

            pick_first(0, lg, e1, s1)
            st(STT(lg2, s1, -3e38, lg, ALU.mult, ALU.add))
            st.wait()
            pick_first(1, lg2, e2, s2)
            TT(top[:, :, 2], top[:, :, 1], top[:, :, 0], ALU.subtract).then_inc(router_diff, 1)
            TT(cs, s1, s2, ALU.add).then_inc(chosen, 1)
            dve.wait_ge(router_exp, 1)
            st(TS(top[:, :, 3], top[:, :, 2], 1.0, None, ALU.add))
            st.wait()
            st(E.reciprocal(w12[:, :, 0], top[:, :, 3]))
            st.wait()
            st(TT(w12[:, :, 1], w12[:, :, 0], top[:, :, 2], ALU.mult))
            dve.wait_ge(ranked, 1)
            cnt, nb, end, start = (R(9 + n)[:, 0, :] for n in range(4))
            st(CP(cnt, bank[5][:, 16:24]))
            st(CP(R(13), bank[5][:, 0:16].rearrange("p (b e) -> p b e", b=2)))
            st.wait()
            st(TS(nb, cnt, float(P), None, ALU.is_gt))
            st.wait()
            st(STT(nb, cnt, 0.0, nb, ALU.is_gt, ALU.add))
            st.wait()
            st(TS(nb[:, 0:1], nb[:, 0:1], 1.0, None, ALU.max))
            st.wait()
            st(E.tensor_tensor_scan(end, nb, nb, 0.0, ALU.add, ALU.bypass))
            st.wait()
            st(TT(start, end, nb, ALU.subtract))
            st.wait()
            for b in range(2):
                st(STT(gs[:, b, :], start, float(P), R(13)[:, b, :], ALU.mult, ALU.add))
            st.wait()
            for n, s in ((0, s1), (1, s2)):
                st(TT(tmp, s, gs, ALU.mult))
                st.wait()
                st(E.tensor_reduce(slot[:, :, n:n + 1], tmp, AX.X, ALU.add))
                st.wait()
            def select():
                for b in range(2):
                    st(TS(oh[:, b, :], iota, slot[:, b, 0:1], None, ALU.is_equal))
                st.wait()
                for b in range(2):
                    ins = STT(sel[:, b, :], iota, slot[:, b, 1:2], oh[:, b, :], ALU.is_equal, ALU.add)
                    if b == 0:
                        st(ins)
                    else:
                        ins.then_inc(sel_ready, 1)
                for b in range(2):
                    st(TS(selw[:, b, :], iota, slot[:, b, 0:1], w12[:, b, 0:1], ALU.is_equal, ALU.mult))
                    st(TS(ow[:, b, :], iota, slot[:, b, 1:2], w12[:, b, 1:2], ALU.is_equal, ALU.mult))
                st.wait()
                TT(selw[:], selw[:], ow[:], ALU.add).then_inc(selw_ready, 1)

            def gathered_lo(first):
                for half in range(2):
                    dve.wait_ge(xh_made, first + half)
                    TT(xl[:, 4 * half:4 * half + 4, :].rearrange("p k s -> p (k s)"), bank[4 + half][:],
                       xh[:, 4 * half:4 * half + 4, :].rearrange("p k s -> p (k s)").bitcast(F32),
                       ALU.subtract).then_inc(xl_made, 1)

            select()
            ended = iit[:].rearrange("p (n e) -> p n e", e=NE)
            st(TT(ended, MC[0:1, 0:16].rearrange("p (n o) -> p n o", o=1).broadcast_to([1, 16, NE]),
                  end[0:1, :].rearrange("p (o e) -> p o e", o=1).broadcast_to([1, 16, NE]), ALU.is_ge))
            st.wait()
            st(E.tensor_reduce(item_f[:], ended, AX.X, ALU.add))
            st.wait()
            TS(it_i[:], item_f[:], float(NE - 1), None, ALU.min).then_inc(items_ready, 1)
            st(CP(nit_i[:, 0:1], end[0:1, NE - 1:NE]))
            TS(nit_i[:, 1:2], end[0:1, NE - 1:NE], 1.0, None, ALU.subtract).then_inc(items_ready, 1)
            dve.sem_inc(h_made, 2)
            dve.sem_inc(hl_made, 2)
            dve.wait_ge(items_ready, 2)
            n_items = dve.value_load(nit_i[0:1, 0:1], min_val=1, max_val=12)
            for k in range(MLOOK - 1):
                if k == 2:
                    gathered_lo(1)
                expert_lo(k, k + 1)
            with dve.Fori(0, n_items) as i:
                expert_lo(MLOOK - 1, i * ITEM + MLOOK)
                m = 0

                def own(ins):
                    nonlocal m
                    ins.then_inc(item_step, 1)
                    m += 1

                def own_wait():
                    dve.wait_ge(item_step, i * OWN + m)

                for k in range(ITEM):
                    dve.wait_ge(chunk_done, i * ITEM + (k + 1))
                    if k % 2 == 1 and k < 2 * N_GU:
                        j = k // 2
                        dve.wait_ge(sg_made, i * N_GU + (j + 1))
                        dve.wait_ge(hl_made, i * N_GU + (j + 1))
                        TT(hs[:, j % 2, :], sg[:, j % 2, :], bank[j % 2][:, EC:2 * EC], ALU.mult).then_inc(h_made, 1)
                    if k % 2 == 0 and 4 <= k <= 2 * N_GU + 2:
                        j = (k - 4) // 2
                        dve.wait_ge(hh_made, i * N_GU + (j + 1))
                        TT(hl[:, 2 * j:2 * j + 2, :].rearrange("p f s -> p (f s)"), bank[6 + j % 2][:, 0:2 * P],
                           hh[:, 2 * j:2 * j + 2, :].rearrange("p f s -> p (f s)").bitcast(F32),
                           ALU.subtract).then_inc(hl_made, 1)
                    if k in (COMBINE_AT + 1, COMBINE_AT + 3):
                        for q in range(k - COMBINE_AT - 1, k - COMBINE_AT + 1):
                            dve.wait_ge(combined, i * 4 + (q + 1))
                            a = acc[:, q // 2, (q % 2) * 512:(q % 2 + 1) * 512]
                            TT(a, a, bank[4 + q % 2][:], ALU.add).then_inc(acc_added, 1)
                    if k == TURN_AT + 1:
                        dve.wait_ge(sel_turned, i + 1)
                        CP(selT[:].rearrange("p b t -> p (b t)"), bank[4][:, 0:2 * P]).then_inc(selT_ready, 1)
                    if k == TURN_AT + 2:
                        own(TS(slot[:, :, 0:2], slot[:, :, 0:2], float(P), None, ALU.subtract))
                        own_wait()
                        for b in range(2):
                            own(TS(oh[:, b, :], iota, slot[:, b, 0:1], None, ALU.is_equal))
                            own(TS(selw[:, b, :], iota, slot[:, b, 0:1], w12[:, b, 0:1], ALU.is_equal, ALU.mult))
                            own(TS(ow[:, b, :], iota, slot[:, b, 1:2], w12[:, b, 1:2], ALU.is_equal, ALU.mult))
                        own_wait()
                        for b in range(2):
                            ins = STT(sel[:, b, :], iota, slot[:, b, 1:2], oh[:, b, :], ALU.is_equal, ALU.add)
                            if b == 0:
                                own(ins)
                            else:
                                ins.then_inc(sel_ready, 1)
                        TT(selw[:], selw[:], ow[:], ALU.add).then_inc(selw_ready, 1)
                    if k == GATHER_AT + 1:
                        gathered_lo(i * 2 + 3)
                    if k < ITEM - 1:
                        expert_lo((k + MLOOK) % ITEM, i * ITEM + (k + MLOOK + 1))
                assert m == OWN
            for q in range(4):
                dve.wait_ge(combined, n_items * 4 + (q + 1))
                a = acc[:, q // 2, (q % 2) * 512:(q % 2 + 1) * 512]
                TT(a, a, bank[4 + q % 2][:], ALU.add).then_inc(acc_added, 1)

        @block.tensor
        def _(pe):
            MM, TR = pe.matmul, pe.transpose

            def norm(phase):
                for k in range(KD) if phase == 0 else (KD - 1,):
                    if phase == 0 and k == 0:
                        pe.wait_ge(h_loaded, KD)
                    ins = sum_squares(phase, k)
                ins.then_inc(norm_sum, 1)

            def sum_squares(phase, m):
                pe.wait_ge(norm_sq, KD * phase + m + 1)
                return MM(bank[2][:, 0:T], ones, gt[:, m, :], start=m == 0, stop=m == KD - 1)

            def product(ps, g, k, row, xh_, xl_, first, last, c0=0):
                h, l = hi[g % HI][:, c0:c0 + P], lo[g % RAW][:, c0:c0 + P]
                MM(ps, h, xh_, start=first, stop=False)
                MM(ps, h, xl_, start=False, stop=False)
                return MM(ps, l, xh_, start=False, stop=last)

            def stream(g, half):
                layer, kind, i = jobs[g]
                j = of_job[g]
                o = j["out"]
                c = live(layer, kind)
                if half == 0:
                    pe.wait_ge(hi_made, g + 1)
                    pe.wait_ge(lo_made, g + 1)
                if kind == "wo":
                    oo = o + half
                    if oo >= 2:
                        drained(pe, oo - 2)
                    if i % 4 == 0 and half == 0:
                        if i == 0:
                            pe.wait_ge(mla_dve, N(layer, "ot", 3, "dve"))
                        else:
                            pe.wait_ge(silu_done, J(layer, "r" if i == 4 else "hg", 3)["silu"] + 1)
                    for k in range(4):
                        ins = product(bank[oo % 2][:, c], g, k, k, OH[:, k, c], OL[:, k, c], k == 0, k == 3,
                                      k * 256 + half * P)
                    ins.then_inc(stream_done, 1)
                    return
                n = tile_source(layer, kind, i)[1][0]
                first = kind != "fd" or i % 3 == 0
                last = kind != "fd" or i % 3 == 2
                if half == 0 and first and o >= 2:
                    drained(pe, o - 2)
                if kind == "fd" and i == 0 and half == 0:
                    pe.wait_ge(silu_done, J(layer, "fu", NF - 1)["silu"] + 1)
                for k in range(*((0, 4) if half == 0 else (4, n))):
                    if kind == "fd":
                        f = 8 * (i % 3) + k
                        xx = HH[:, f, :], HL[:, f, :]
                    else:
                        if g in need_u:
                            pe.wait_ge(u_ready, 8 * need_u[g] + k + 1)
                        xx = UH[:, k, c], UL[:, k, c]
                    ins = product(bank[o % 2][:, c], g, k, k, *xx, first and k == 0, last and k == n - 1, k * P)
                if half == 1:
                    ins.then_inc(stream_done, 1)

            def mla(layer, name, i):
                p = i % 2
                Ma, Mb = bank[2 + 2 * p], bank[3 + 2 * p]
                if name == "ss":
                    drained(pe, J(layer, "dkv", 0)["out"])
                    drained(pe, J(layer, "dkv", 0)["out"] - 1)
                    MM(bank[2][:, 0:T], ones, gt[:, 0, :], start=True, stop=False)
                    MM(bank[2][:, 0:T], ones, gt[:, 1, :], start=False, stop=True)
                    MM(bank[3][:, 0:T], ones, gt[:, 2, :], start=True, stop=True).then_inc(mla_psum, 1)
                elif name == "vm":
                    pe.wait_ge(mla_dve, N(layer, "ss", 0, "dve"))
                    pe.wait_ge(small_landed, 48 * (layer + 1))
                    vw = wukv[:].rearrange("p (h c) -> p h c", h=HEADS)[:, :, NOPE:]
                    for b, (c0, n) in enumerate(BLOCKS):
                        ins = MM(bank[(4, 5, 2)[b]][0:n, :].rearrange("p (h c) -> p h c", h=HEADS),
                                 dqT[:, 2, c0:c0 + n], vw, start=True, stop=True)
                    ins.then_inc(mla_psum, 1)
                elif name == "qk":
                    if i < 2:
                        pe.wait_ge(mla_act, N(layer, "vm", 0, "act"))
                    else:
                        pe.wait_ge(mla_dve, N(layer, "pv", i - 2, "dve"))
                    for t in range(2):
                        MM(Ma[0:QK, 0:T], wuq[:, t, i * QK:(i + 1) * QK], dqT[:, t, :], start=t == 0, stop=t == 1)
                    MM(Mb[0:NOPE, 0:T], wukv[:, i * P:i * P + NOPE], dqT[:, 2, :],
                       start=True, stop=True).then_inc(mla_psum, 1)
                elif name == "nrm":
                    pe.wait_ge(mla_act, N(layer, "qk", i, "act"))
                    pe.wait_ge(mla_dve, N(layer, "qk", i, "dve"))
                    MM(Ma[0:QK, 0:T], ones[0:QK, 0:QK], qsq[:, p, 0, :], start=True, stop=True)
                    MM(Mb[0:QK, 0:T], ones[0:QK, 0:QK], qsq[:, p, 1, :], start=True, stop=True).then_inc(mla_psum, 1)
                elif name == "rot":
                    pe.wait_ge(mla_dve, N(layer, "nrm", i, "dve"))
                    R_ = C[NOPE:QK, cc["rot"]]
                    MM(Ma[NOPE:QK, 0:T], R_, qk[NOPE:QK, p, 0, :], start=True, stop=True)
                    MM(Mb[NOPE:QK, 0:T], R_, qk[NOPE:QK, p, 1, :], start=True, stop=True).then_inc(mla_psum, 1)
                elif name == "sc":
                    pe.wait_ge(mla_dve, N(layer, "rot", i, "dve"))
                    q_, k_ = qk[:, p, 0, :], qk[:, p, 1, :]
                    MM(Ma[:, 0:272], q_[:, 144:272], k_, start=True, stop=True)
                    MM(Ma[:, 272:416], q_[:, 16:144], k_[:, 0:144], start=True, stop=True)
                    MM(Ma[0:META, 416:432], q_[:, 0:16], k_[:, 0:16], start=True, stop=True).then_inc(mla_psum, 1)
                elif name == "pt":
                    pe.wait_ge(mla_act, N(layer, "sc", i, "act"))
                    TR(Mb[:, 0:128], pr[:, p, 16:144], ident)
                    TR(Mb[:, 128:256], pr[:, p, 144:272], ident)
                    TR(Mb[:, 256:384], pr[:, p, 288:416], ident)
                    TR(Ma[0:META, 0:128], pr[:, p, 0:16], ident)
                    TR(Ma[0:META, 128:256], pr[:, p, 272:288], ident)
                    TR(Ma[0:META, 256:272], pr[0:META, p, 416:432], ident[0:META, 0:META]).then_inc(mla_psum, 1)
                elif name == "pv":
                    pe.wait_ge(mla_act, N(layer, "pt", i, "act"))
                    pe.wait_ge(mla_dve, N(layer, "pt", i, "dve"))
                    c = slice(i * VDIM, (i + 1) * VDIM)
                    MM(Ma[:, 0:VDIM], ptm[:, p, 0:128], vtok[0:META, 0, c], start=True, stop=False)
                    MM(Ma[:, 0:VDIM], ptf[:, p, 0:128], vtok[:, 1, c], start=False, stop=False)
                    MM(Ma[:, 0:VDIM], ptf[:, p, 128:256], vtok[:, 2, c], start=False, stop=True)
                    MM(Mb[:, 0:VDIM], ptm[:, p, 128:256], vtok[0:META, 0, c], start=True, stop=False)
                    MM(Mb[:, 0:VDIM], ptf[:, p, 256:384], vtok[:, 1, c], start=False, stop=True)
                    MM(Mb[0:META, VDIM:2 * VDIM], ptm[:, p, 256:272], vtok[0:META, 0, c],
                       start=True, stop=True).then_inc(mla_psum, 1)
                elif name == "ot":
                    pe.wait_ge(mla_dve, N(layer, "pv", HEADS - 1, "dve"))
                    M, c = bank[2 + i], slice(i * P, (i + 1) * P)
                    TR(M[:, 16:144], otok[:, 1, c], ident)
                    TR(M[:, 144:272], otok[:, 2, c], ident)
                    TR(M[:, 0:16], otok[0:META, 0, c], ident[0:META, 0:META]).then_inc(mla_psum, 1)

            def la(unit, name, i):
                layer, u = divmod(unit, 3)
                L = bank[6 + i % 2]
                nh = heads_of(unit)
                if name == "gz":
                    drained(pe, J(layer, "gd", 0)["out"])
                    pe.wait_ge(small_landed, 48 * (layer + 1))
                    if layer:
                        pe.wait_ge(la_dve, N(unit - 1, "n", 1, "dve"))
                    for t in range(2):
                        ins = MM(bank[6 + t][:, 0:T], wg2[:, t * P:(t + 1) * P], gdT[:], start=True, stop=True)
                    ins.then_inc(la_psum, 1)
                elif name == "vt":
                    if i == 0:
                        o = J(layer, "v", 3 if u == 0 else 5 + 2 * (u - 1))["out"]
                        drained(pe, o)
                        drained(pe, o - 1)
                    if u == 0 and i < 2:
                        pe.wait_ge(la_dve, N(unit, "gz", 0, "dve"))
                    elif i >= 2:
                        pe.wait_ge(la_act, N(unit, "vt", i - 2, "act"))
                    else:
                        pe.wait_ge(la_act, N(unit - 1, "n", heads_of(unit - 1) - 2 + i, "act"))
                    _, c = chunk_cols(i)
                    rows = c.stop - c.start
                    for h in range(nh):
                        ins = TR(L[0:rows, h * P:(h + 1) * P], VT[:, h, c], ident)
                    ins.then_inc(la_psum, 1)
                elif name == "kt":
                    pe.wait_ge(la_act, N(unit, "vt", 4 if i == 0 else 3, "act"))
                    pe.wait_ge(la_dve, N(unit, "mul3", 0, "dve"))
                    for c in (2 * i, 2 * i + 1):
                        cols, _ = chunk_cols(c)
                        rows = cols.stop - cols.start
                        for t in range(2):
                            ins = TR(L[0:rows, (c % 2) * 256 + t * P:(c % 2) * 256 + (t + 1) * P], K[:, t, cols], ident)
                    ins.then_inc(la_psum, 1)
                elif name == "ds":
                    pe.wait_ge(la_dve, N(unit, "kt", 1, "dve"))
                    pe.wait_ge(la_act, N(unit, "vt", 4, "act"))
                    where = [(2 * i, 0, 64), (2 * i + 1, 64, 128)] if u == 0 else [(i, 0, 128)]
                    for c in range(4):
                        rows = META if c == 0 else CH
                        for h, a, b in where:
                            ins = MM(L[a:b, c * P:(c + 1) * P], KLT[0:rows, c, i * P + a:i * P + b],
                                     V[0:rows, c, h * P:(h + 1) * P], start=True, stop=True)
                    ins.then_inc(la_psum, 1)
                elif name == "a":
                    if i < 2:
                        pe.wait_ge(la_dve, N(unit, "ds", 1, "dve"))
                    else:
                        pe.wait_ge(la_act, N(unit, "n", i - 2, "act"))
                    t, a, b = (i // 2, 64 * (i % 2), 64 * (i % 2) + 64) if u == 0 else (i, 0, P)
                    for c in range(1, NCH):
                        MM(L[0:CH, (c - 1) * CH:c * CH], KE[a:b, t, c * CH:(c + 1) * CH],
                           QE[a:b, t, c * CH:(c + 1) * CH], start=True, stop=True)
                    MM(L[0:META, 256:272], KE[a:b, t, OFF:CH], QE[a:b, t, OFF:CH],
                       start=True, stop=True).then_inc(la_psum, 1)
                elif name == "o":
                    pe.wait_ge(la_dve, N(unit, "a", i, "dve"))
                    t = i // 2 if u == 0 else i
                    v = lambda c, rows: V[0:rows, c, i * P:(i + 1) * P]
                    MM(L[:, 0:META], v(0, META), AT[0:META, i % 2, 256:272], start=True, stop=True)
                    for c in range(1, NCH):
                        ps = L[:, META + (c - 1) * CH:META + c * CH]
                        MM(ps, v(c, CH), AT[:, i % 2, (c - 1) * CH:c * CH], start=True, stop=False)
                        ins = MM(ps, S[:, c - 1, i, :], Q[:, t, c * CH:(c + 1) * CH], start=False, stop=True)
                    ins.then_inc(la_psum, 1)
                elif name == "n":
                    pe.wait_ge(la_act, N(unit, "o", i, "act"))
                    MM(L[:, 0:T], ones, osq[:, i % 2, :], start=True, stop=True).then_inc(la_psum, 1)

            pe.wait_ge(meta_landed, 32)
            for k in range(KD):
                if k % 4 == 0:
                    pe.wait_ge(x_landed[k // 4], 16)
                if k >= 2:
                    pe.wait_ge(h_loaded, k - 1)
                b_ = bank[2 + k % 2]
                TR(b_[:, 16:144], x_in[:, 0, k * P:(k + 1) * P], ident)
                TR(b_[:, 144:272], x_in[:, 1, k * P:(k + 1) * P], ident)
                TR(b_[:, 0:16], vtok[0:META, k // 4, (k % 4) * P:(k % 4 + 1) * P],
                   ident[0:META, 0:META]).then_inc(x_turned, 1)
            pe.wait_ge(zeroed, 1)
            norm(0)
            pe.wait_ge(const_landed, 16)
            phase = 1
            for g in range(NG):
                if g in norm_before:
                    norm(phase)
                    phase += 1
                for half in range(2):
                    stream(g, half)
                    if half == 1 and g in squares_at:
                        sum_squares(*squares_at[g])
                    for s in shares["pe"].get(2 * g + half, ()):
                        if s[1] in PE_PART:
                            (mla if s[1] in MLA_NAMES else la)(*s)

            norm(phase)
            pe.wait_ge(moe_const, 48)
            for k in range(KD):
                pe.wait_ge(u_whole, KD * phase + k + 1)
                ins = MM(bank[4][0:NE, 0:SEQ], wr[:, k, :], mixed[:, k, META:T], start=k == 0, stop=k == KD - 1)
            ins.then_inc(logits_ready, 1)
            for b in range(2):
                for half in range(2):
                    if b:
                        pe.wait_ge(utok_made, half + 1)
                        pe.wait_ge(acc_loaded, half + 1)
                    for src, bk, done in ((mixed, bank[half], turned_u), (hT, bank[2 + half], turned_h)):
                        for k in range(4):
                            ins = TR(bk[:, k * P:(k + 1) * P], src[:, 4 * half + k, META + b * P:META + (b + 1) * P], ident)
                        ins.then_inc(done, 1)
                        if b == 0 and half == 0 and src is mixed:
                            pe.wait_ge(logits_moved, 1)
                            for t in range(2):
                                ins = TR(bank[5][:, 32 + 8 * t:40 + 8 * t], oh[0:NE, t, :], ident[0:NE, 0:NE])
                            ins.then_inc(logits_ready, 1)
            pe.wait_ge(chosen, 1)
            cs = rt[:, 6, :, :]
            MM(bank[5][:, 0:8], tri, cs[:, 0, :], start=True, stop=True)
            for c0, last_w in ((8, tri), (16, ones)):
                MM(bank[5][:, c0:c0 + 8], ones, cs[:, 0, :], start=True, stop=False)
                ins = MM(bank[5][:, c0:c0 + 8], last_w, cs[:, 1, :], start=False, stop=True)
            ins.then_inc(ranked, 1)
            def gather():
                for half in range(2):
                    for k in range(4):
                        for b in range(2):
                            c0 = (4 * half + k) * P
                            ins = MM(bank[4 + half][:, k * P:(k + 1) * P], utok[:, b, c0:c0 + P], sel[:, b, :],
                                     start=b == 0, stop=b == 1)
                    ins.then_inc(x_gathered, 1)

            def combine(q):
                return MM(bank[4 + q % 2][:], selT[:, q // 2, :], ys[:, (q % 2) * 512:(q % 2 + 1) * 512],
                          start=True, stop=True).then_inc(combined, 1)

            pe.wait_ge(utok_made, 4)
            pe.wait_ge(acc_loaded, 4)
            pe.wait_ge(sel_ready, 1)
            pe.wait_ge(zeroed, 2)
            gather()
            pe.wait_ge(items_ready, 2)
            n_items = pe.value_load(nit_i[0:1, 0:1], min_val=1, max_val=12)
            with pe.Fori(0, n_items) as i:
                for k in range(ITEM):
                    pe.wait_ge(mhi_made, i * ITEM + (k + 1))
                    pe.wait_ge(mlo_made, i * ITEM + (k + 1))
                    h, l = mhi[k % MHI], mlo[k % MRAW]
                    if k < 2 * N_GU:
                        j = k // 2
                        if k == 0:
                            pe.wait_ge(xl_made, i * 2 + 2)
                        if k % 2 == 0:
                            pe.wait_ge(h_made, i * N_GU + (j + 1))
                        ps = bank[j % 2][:, (k % 2) * EC:(k % 2 + 1) * EC]
                        for r in range(KD):
                            c = slice(r * EC, (r + 1) * EC)
                            MM(ps, xh[:, r, :], h[:, c], start=r == 0, stop=False)
                            MM(ps, xh[:, r, :], l[:, c], start=False, stop=False)
                            ins = MM(ps, xl[:, r, :], h[:, c], start=False, stop=r == KD - 1)
                    else:
                        d = k - 2 * N_GU
                        pe.wait_ge(hl_made, i * N_GU + (d + 3))
                        if d == 0:
                            pe.wait_ge(y_out, i * 2 + 2)
                        for f in range(2):
                            for n in range(2):
                                c = slice(f * D + n * 512, f * D + (n + 1) * 512)
                                ps = bank[2 + n][:]
                                MM(ps, hh[:, 2 * d + f, :], h[:, c], start=d == 0 and f == 0, stop=False)
                                MM(ps, hh[:, 2 * d + f, :], l[:, c], start=False, stop=False)
                                ins = MM(ps, hl[:, 2 * d + f, :], h[:, c], start=False, stop=d == N_DN - 1 and f == 1)
                    ins.then_inc(chunk_done, 1)
                    if k % 2 == 1 and 3 <= k <= 2 * N_GU + 1:
                        j = (k - 3) // 2
                        pe.wait_ge(h_made, i * N_GU + (j + 3))
                        pe.wait_ge(hl_made, i * N_GU + (j + 1))
                        for f in range(2):
                            ins = TR(bank[6 + j % 2][:, f * P:(f + 1) * P], hs[:, j % 2, f * P:(f + 1) * P], ident)
                        ins.then_inc(h_turned, 1)
                    if k == COMBINE_AT:
                        pe.wait_ge(y_out, i * 2 + 2)
                        for q in range(2):
                            combine(q)
                    if k == COMBINE_AT + 2:
                        for q in range(2, 4):
                            pe.wait_ge(acc_added, i * 4 + (q - 1))
                            combine(q)
                    if k == TURN_AT:
                        pe.wait_ge(acc_added, i * 4 + 4)
                        pe.wait_ge(selw_ready, i + 1)
                        for b in range(2):
                            ins = TR(bank[4][:, b * P:(b + 1) * P], selw[:, b, :], ident)
                        ins.then_inc(sel_turned, 1)
                    if k == GATHER_AT:
                        pe.wait_ge(sel_ready, i + 2)
                        pe.wait_ge(selT_ready, i + 1)
                        gather()
            pe.wait_ge(y_out, n_items * 2 + 2)
            pe.wait_ge(xl_made, n_items * 2 + 2)
            for q in range(4):
                if q >= 2:
                    pe.wait_ge(acc_added, n_items * 4 + (q - 1))
                combine(q)


CONSTS = [("ident", P), ("ones", P), ("rot", ROPE), ("cos", T), ("sin", T), ("smask", 432),
          ("reset", LP)]


def constants():
    c = {n: np.zeros((P, w), np.float32) for n, w in CONSTS}
    p = np.arange(P)
    c["ident"][p, p] = 1
    c["ones"][:] = 1
    half = ROPE // 2
    for j in range(half):
        c["rot"][NOPE + half + j, j] = -1
        c["rot"][NOPE + j, half + j] = 1
    inv = np.float32(10000.0) ** (-np.arange(half, dtype=np.float32) / np.float32(half))
    ang = np.arange(T, dtype=np.float32)[None, :] * inv[:, None].astype(np.float32)
    c["cos"][NOPE:QK] = np.concatenate([np.cos(ang)] * 2)
    c["sin"][NOPE:QK] = np.concatenate([np.sin(ang)] * 2)
    for c0, q0, n in ((0, META + P, T), (T, META, META + P), (T + META + P, 0, META)):
        c["smask"][:, c0:c0 + n] = np.where(np.arange(n)[None, :] <= q0 + p[:, None], 0, NEG)
    j, i = np.arange(CH)[:, None], np.arange(CH)[None, :]
    c["cos"][0:CH, 0:256] = np.tile(j <= i, (1, 4))
    c["cos"][0:META, 256:272] = (j <= i)[0:META, 0:META]
    c["reset"][:] = (np.arange(LP) % CH != 0)[None, :]
    out = np.concatenate([c[n] for n, _ in CONSTS], 1).astype(np.float32)
    moe = np.concatenate([np.tile(np.arange(P)[None, :], (P, 1)), p[:, None] < p[None, :],
                          np.zeros((P, P))], 1).astype(np.float32)
    return out, moe


WEIGHTS = ["w_in", "w_mla_uq", "w_mla_ukv", "w_gla_g2", "w_mla_o", "w_gla_o", "w_hgrn_o", "w_out", "w_ff_gate",
           "w_ff_up", "w_ff_down", "w_router", "b_router", "w_exp_gate", "w_exp_up", "w_exp_down"]


def lay_out(a):
    ins = {n: np.ascontiguousarray(a[n]) for n in WEIGHTS + ["x", "meta_tokens"]}
    par = np.zeros((P, DEPTH, NPAR), np.float32)
    src = dict(attn="attn_norm", ffn="ffn_norm", cq="mla_cq_norm", ckv="mla_ckv_norm", qn="mla_q_norm",
               kn="mla_k_norm", bg="b_gla_g", glao="gla_o_norm", hgrno="hgrn_o_norm", lb="hgrn_lower_bounds")
    for name, key in src.items():
        v = np.asarray(a[key])
        for layer in range(DEPTH):
            rows = min(P, v.shape[1])
            cols = v[layer].reshape(-1, rows).T
            par[0:rows, layer, PCOL[name]:PCOL[name] + cols.shape[1]] = cols
    ins["params"] = par
    ins["consts"], ins["moe_consts"] = constants()
    return ins


def kernel(**inputs):
    import concourse.bacc as _bacc
    from concourse.bass_utils import run_bass_kernel_spmd as _run

    nc = _bacc.Bacc("TRN2", target_bir_lowering=False, num_devices=1)
    arrays = {f"in_{n}": a for n, a in lay_out(inputs).items()}
    A = {n[3:]: nc.dram_tensor(n, a.shape, mybir.dt.from_np(a.dtype), kind="ExternalInput").ap()
         for n, a in arrays.items()}
    out = nc.dram_tensor("out", (1, SEQ, D), F32, kind="ExternalOutput").ap()
    bass_hybrid_trunk(nc, A, out)
    return _run(nc, [arrays], core_ids=[0]).results[0]["out"]
```
